# Optimizing a Trainium2 kernel written in Bass

```python
import jax, jax.numpy as jnp
from jax import lax
import numpy as np

D_MODEL = 1024
BATCH = 1
SEQ = 512
DEPTH = 1

GRID_W = 64
NA_WIDTH = D_MODEL // 2
NA_HEADS = 8
NA_HEAD_DIM = NA_WIDTH // NA_HEADS
WIN_ROWS_MAX = 8
WIN_COLS = 16
POOL_WIDTH = D_MODEL - NA_WIDTH
POOL_WINDOWS = (2, 4, 8, 16)
POOL_GROUPS = len(POOL_WINDOWS)
POOL_GROUP_DIM = POOL_WIDTH // POOL_GROUPS
MIX_WIDTH = NA_WIDTH + POOL_WIDTH
IN_WIDTH = 3 * NA_WIDTH + POOL_WIDTH
D_FF = -(-8 * D_MODEL // (3 * 256)) * 256
EPS = 1e-6


def rms_norm(x, g):
    xf = x.astype(jnp.float32)
    y = xf * lax.rsqrt(jnp.mean(xf * xf, axis=-1, keepdims=True) + EPS)
    return (y * g.astype(jnp.float32)).astype(x.dtype)

def neighbourhood_attention(q, k, v, rpb):
    B, T, H, Dh = q.shape
    rows = T // GRID_W
    wr = min(WIN_ROWS_MAX, rows)
    q = q.reshape(B, rows, GRID_W, H, Dh)
    k = k.reshape(B, rows, GRID_W, H, Dh)
    v = v.reshape(B, rows, GRID_W, H, Dh)
    row_start = jnp.clip(jnp.arange(rows) - wr // 2, 0, rows - wr)
    cols = jnp.arange(GRID_W)
    col_idx = jnp.clip(cols - WIN_COLS // 2, 0, GRID_W - WIN_COLS)[:, None] + jnp.arange(WIN_COLS)
    col_rel = col_idx - cols[:, None] + (WIN_COLS - 1)
    rpb_cols = rpb.astype(jnp.float32)[:, :, col_rel]
    scale = Dh ** -0.5

    def one_row(r):
        rs = row_start[r]
        kb = lax.dynamic_slice_in_dim(k, rs, wr, axis=1)
        vb = lax.dynamic_slice_in_dim(v, rs, wr, axis=1)
        kg = kb[:, :, col_idx]
        vg = vb[:, :, col_idx]
        qr = lax.dynamic_index_in_dim(q, r, axis=1, keepdims=False)
        row_rel = rs + jnp.arange(wr) - r + (WIN_ROWS_MAX - 1)
        bias = jnp.transpose(rpb_cols[:, row_rel], (0, 2, 1, 3))
        s = jnp.einsum('bqhd,bwqkhd->bhqwk', qr, kg,
                       preferred_element_type=jnp.float32) * scale + bias[None]
        p = jax.nn.softmax(s.reshape(B, H, GRID_W, wr * WIN_COLS), axis=-1)
        p = p.reshape(B, H, GRID_W, wr, WIN_COLS).astype(v.dtype)
        return jnp.einsum('bhqwk,bwqkhd->bqhd', p, vg)

    out = lax.map(one_row, jnp.arange(rows))
    return jnp.moveaxis(out, 0, 1).reshape(B, T, H * Dh)

def multiscale_pool(u, w_pool, pool_scale):
    B, T, C = u.shape
    uf = u.astype(jnp.float32)
    csum = jnp.concatenate([jnp.zeros((B, 1, C), jnp.float32), jnp.cumsum(uf, axis=1)], axis=1)
    t = jnp.arange(T)
    outs = []
    for g, w in enumerate(POOL_WINDOWS):
        sl = slice(g * POOL_GROUP_DIM, (g + 1) * POOL_GROUP_DIM)
        lo = jnp.clip(t - w // 2, 0, T)
        hi = jnp.clip(t + w // 2, 0, T)
        cg = csum[:, :, sl]
        mean = (cg[:, hi] - cg[:, lo]) / (hi - lo).astype(jnp.float32)[:, None]
        outs.append(mean - uf[:, :, sl])
    d = jnp.stack(outs, axis=2).astype(u.dtype)
    y = jnp.einsum('btgc,gcd->btgd', d, w_pool).reshape(B, T, C)
    return y * pool_scale

def first_inputs(seed: int = 0) -> dict:
    key = jax.random.key(seed)
    ks = jax.random.split(key, 14)
    f32 = jnp.float32
    nrm = lambda k, shape, fan_in: jax.random.normal(k, shape, f32) * fan_in ** -0.5
    gain = lambda k, shape: 1.0 + 0.02 * jax.random.normal(k, shape, f32)
    return {
        "x": jax.random.normal(ks[0], (BATCH, SEQ, D_MODEL), f32),
        "norm1_g": gain(ks[1], (DEPTH, D_MODEL)),
        "w_in": nrm(ks[2], (DEPTH, D_MODEL, IN_WIDTH), D_MODEL),
        "q_norm_g": gain(ks[3], (DEPTH, NA_HEAD_DIM)),
        "k_norm_g": gain(ks[4], (DEPTH, NA_HEAD_DIM)),
        "rpb": 0.1 * jax.random.normal(ks[5], (DEPTH, NA_HEADS, 2 * WIN_ROWS_MAX - 1, 2 * WIN_COLS - 1), f32),
        "w_pool": nrm(ks[6], (DEPTH, POOL_GROUPS, POOL_GROUP_DIM, POOL_GROUP_DIM), POOL_GROUP_DIM),
        "pool_scale": gain(ks[7], (DEPTH, POOL_WIDTH)),
        "w_out": nrm(ks[8], (DEPTH, MIX_WIDTH, D_MODEL), MIX_WIDTH),
        "norm2_g": gain(ks[9], (DEPTH, D_MODEL)),
        "w_gate": nrm(ks[10], (DEPTH, D_MODEL, D_FF), D_MODEL),
        "w_up": nrm(ks[11], (DEPTH, D_MODEL, D_FF), D_MODEL),
        "w_down": nrm(ks[12], (DEPTH, D_FF, D_MODEL), D_FF),
    }

def first_block(x, norm1_g, w_in, q_norm_g, k_norm_g, rpb, w_pool, pool_scale, w_out,
              norm2_g, w_gate, w_up, w_down):
    B, T, _ = x.shape
    for l in range(DEPTH):
        h = rms_norm(x, norm1_g[l])
        proj = h @ w_in[l]
        q = proj[..., :NA_WIDTH].reshape(B, T, NA_HEADS, NA_HEAD_DIM)
        k = proj[..., NA_WIDTH:2 * NA_WIDTH].reshape(B, T, NA_HEADS, NA_HEAD_DIM)
        v = proj[..., 2 * NA_WIDTH:3 * NA_WIDTH].reshape(B, T, NA_HEADS, NA_HEAD_DIM)
        u = proj[..., 3 * NA_WIDTH:]
        q = rms_norm(q, q_norm_g[l])
        k = rms_norm(k, k_norm_g[l])
        a = neighbourhood_attention(q, k, v, rpb[l])
        p = multiscale_pool(u, w_pool[l], pool_scale[l])
        x = x + jnp.concatenate([a, p], axis=-1) @ w_out[l]
        h2 = rms_norm(x, norm2_g[l])
        x = x + (jax.nn.silu(h2 @ w_gate[l]) * (h2 @ w_up[l])) @ w_down[l]
    return x


HEAD_DIM = 64
N_HEADS = 8
N_KV_HEADS = 2
GROUP = N_HEADS // N_KV_HEADS
WINDOW = 128
BLOCK = 128
ATTN_SCALE = HEAD_DIM ** -0.5
ATTN_WIDTH = N_HEADS * HEAD_DIM
KV_WIDTH = N_KV_HEADS * HEAD_DIM
CONV_GROUPS = 8
CONV_WIDTH = CONV_GROUPS * 64
CONV_K = 3
IN_WIDTH_2 = ATTN_WIDTH + 2 * KV_WIDTH + 3 * CONV_WIDTH + 2 * D_MODEL
D_FF_2 = 2816
FFN_CONV_K = 3
NORM_EPS = 1e-5


def rms_norm_2(x, g):
    xf = x.astype(jnp.float32)
    y = xf * lax.rsqrt(jnp.mean(xf * xf, axis=-1, keepdims=True) + NORM_EPS)
    return (y * g.astype(jnp.float32)).astype(x.dtype)

def causal_depthwise_conv(x, w):
    k_width, ch = w.shape
    return lax.conv_general_dilated(
        x, w[:, None, :].astype(x.dtype), window_strides=(1,), padding=((k_width - 1, 0),),
        dimension_numbers=("NWC", "WIO", "NWC"), feature_group_count=ch)

def sliding_window_attention(q, k, v, sinks):
    b, s, _ = q.shape
    nb = s // BLOCK
    q = q.reshape(b, nb, BLOCK, N_KV_HEADS, GROUP, HEAD_DIM)
    k = k.reshape(b, nb, BLOCK, N_KV_HEADS, HEAD_DIM)
    v = v.reshape(b, nb, BLOCK, N_KV_HEADS, HEAD_DIM)

    def with_prev(t):
        prev = jnp.pad(t, ((0, 0), (1, 0), (0, 0), (0, 0), (0, 0)))[:, :-1]
        return jnp.concatenate([prev, t], axis=2)

    kw, vw = with_prev(k), with_prev(v)
    scores = jnp.einsum("bnqhgd,bnkhd->bnhgqk", q, kw).astype(jnp.float32) * ATTN_SCALE
    qi = jnp.arange(BLOCK)[:, None]
    kj = jnp.arange(2 * BLOCK)[None, :]
    dist = qi + BLOCK - kj
    band = (dist >= 0) & (dist < WINDOW)
    real = (jnp.arange(nb)[:, None, None] > 0) | (kj[None] >= BLOCK)
    mask = band[None] & real
    scores = jnp.where(mask[None, :, None, None], scores, -jnp.inf)
    sink = jnp.broadcast_to(sinks.astype(jnp.float32).reshape(1, 1, N_KV_HEADS, GROUP, 1, 1),
                            scores.shape[:-1] + (1,))
    probs = jax.nn.softmax(jnp.concatenate([scores, sink], axis=-1), axis=-1)[..., :-1]
    out = jnp.einsum("bnhgqk,bnkhd->bnqhgd", probs.astype(v.dtype), vw)
    return out.reshape(b, s, ATTN_WIDTH)

def second_inputs(seed: int = 0) -> dict:
    key = jax.random.key(seed)
    ks = jax.random.split(key, 16)
    f32 = jnp.float32

    def nrm(k, shape, scale):
        return jax.random.normal(k, shape, f32) * scale

    return {
        "x": nrm(ks[0], (BATCH, SEQ, D_MODEL), 1.0),
        "mix_norm": 1.0 + nrm(ks[1], (DEPTH, D_MODEL), 0.02),
        "w_in": nrm(ks[2], (DEPTH, D_MODEL, IN_WIDTH_2), D_MODEL ** -0.5),
        "b_in": nrm(ks[3], (DEPTH, IN_WIDTH_2), 0.02),
        "sinks": nrm(ks[4], (DEPTH, N_HEADS), 0.5),
        "conv_w": nrm(ks[5], (DEPTH, CONV_K, CONV_WIDTH), CONV_K ** -0.5),
        "w_attn_branch": nrm(ks[6], (DEPTH, ATTN_WIDTH, D_MODEL), ATTN_WIDTH ** -0.5),
        "w_conv_branch": nrm(ks[7], (DEPTH, CONV_WIDTH, D_MODEL), CONV_WIDTH ** -0.5),
        "w_out": nrm(ks[8], (DEPTH, D_MODEL, D_MODEL), D_MODEL ** -0.5),
        "ffn_norm": 1.0 + nrm(ks[9], (DEPTH, D_MODEL), 0.02),
        "w_up": nrm(ks[10], (DEPTH, D_MODEL, 2 * D_FF_2), D_MODEL ** -0.5),
        "ffn_conv_w": nrm(ks[11], (DEPTH, FFN_CONV_K, 2 * D_FF_2), FFN_CONV_K ** -0.5),
        "w_down": nrm(ks[12], (DEPTH, D_FF_2, D_MODEL), D_FF_2 ** -0.5),
        "final_norm": 1.0 + nrm(ks[13], (D_MODEL,), 0.02),
    }

def second_block(x, mix_norm, w_in, b_in, sinks, conv_w, w_attn_branch, w_conv_branch, w_out,
              ffn_norm, w_up, ffn_conv_w, w_down, final_norm):
    h = x
    splits = np.cumsum([ATTN_WIDTH, KV_WIDTH, KV_WIDTH, CONV_WIDTH, CONV_WIDTH, CONV_WIDTH, D_MODEL])
    for l in range(DEPTH):
        xn = rms_norm_2(h, mix_norm[l])
        proj = jnp.einsum("bsd,dp->bsp", xn, w_in[l]) + b_in[l]
        q, k, v, cb, cc, cx, ga, gc = jnp.split(proj, splits, axis=-1)
        attn = sliding_window_attention(q, k, v, sinks[l])
        conv = cb * causal_depthwise_conv(cc * cx, conv_w[l])
        merged = (jax.nn.sigmoid(ga) * jnp.einsum("bsc,cd->bsd", attn, w_attn_branch[l])
                  + jax.nn.sigmoid(gc) * jnp.einsum("bsc,cd->bsd", conv, w_conv_branch[l]))
        h = h + jnp.einsum("bsd,de->bse", merged, w_out[l])
        hn = rms_norm_2(h, ffn_norm[l])
        up = causal_depthwise_conv(jnp.einsum("bsd,df->bsf", hn, w_up[l]), ffn_conv_w[l])
        gate, val = jnp.split(up, 2, axis=-1)
        h = h + jnp.einsum("bsf,fd->bsd", jax.nn.silu(gate) * val, w_down[l])
    return rms_norm_2(h, final_norm)


def setup_inputs(seed=0):
    out = dict(first_inputs(seed))
    for name, value in second_inputs(seed + 1).items():
        if name != "x":
            out[name + "_2"] = value
    return out


def reference(
    x, norm1_g, w_in, q_norm_g, k_norm_g, rpb, w_pool, pool_scale, w_out, norm2_g, w_gate, w_up,
    w_down, mix_norm_2, w_in_2, b_in_2, sinks_2, conv_w_2, w_attn_branch_2, w_conv_branch_2,
    w_out_2, ffn_norm_2, w_up_2, ffn_conv_w_2, w_down_2, final_norm_2,
):
    x = first_block(
        x, norm1_g, w_in, q_norm_g, k_norm_g, rpb, w_pool, pool_scale, w_out, norm2_g, w_gate,
        w_up, w_down,
    )
    return second_block(
        x, mix_norm_2, w_in_2, b_in_2, sinks_2, conv_w_2, w_attn_branch_2, w_conv_branch_2,
        w_out_2, ffn_norm_2, w_up_2, ffn_conv_w_2, w_down_2, final_norm_2,
    )


_drawn_inputs = setup_inputs


def setup_inputs(seed=0):
    import zlib

    import numpy as np

    out = dict(_drawn_inputs(seed))
    spreads = {}
    factors = {'norm1_g': 3.579,
     'q_norm_g': 8.0,
     'k_norm_g': 8.0,
     'rpb': 5.164,
     'pool_scale': 4.05,
     'norm2_g': 3.542,
     'mix_norm_2': 3.828,
     'b_in_2': 3.375,
     'sinks_2': 64.0,
     'ffn_norm_2': 23.24,
     'final_norm_2': 7.721}
    for name, (base, spread) in spreads.items():
        noise = np.random.default_rng([zlib.crc32(name.encode()), seed]).standard_normal(out[name].shape)
        drawn = base * np.exp(spread * noise) if base else spread * noise
        out[name] = __import__('jax').numpy.asarray(drawn.astype(out[name].dtype))
    for name, factor in factors.items():
        out[name] = (out[name] * factor).astype(out[name].dtype)
    return out
```

```python
from contextlib import ExitStack

import concourse.bass as bass
from concourse import mybir

ALU = mybir.AluOpType
ACT = mybir.ActivationFunctionType
F32 = mybir.dt.float32
F32R = mybir.dt.float32r
AX_X = mybir.AxisListType.X

P = 128
MASKED = -1e30


def two_blocks(
    nc, x, norm1_g, w_in, q_norm_g, k_norm_g, rpb, w_pool, pool_scale, w_out, norm2_g, w_gate, w_up,
    w_down, mix_norm_2, w_in_2, b_in_2, sinks_2, conv_w_2, w_attn_branch_2, w_conv_branch_2,
    w_out_2, ffn_norm_2, w_up_2, ffn_conv_w_2, w_down_2, final_norm_2, out,
):
    T, D = x.shape[1], x.shape[2]
    KC = D // P
    NT = T // P
    F = w_gate.shape[2]
    FC = F // P
    assert (T, D, F, w_up_2.shape[2]) == (512, 1024, 2816, 2 * F)
    HALF = KC * P
    GROUPS = [(g, min(KC, FC - g)) for g in range(0, FC, KC)]
    HEADS, HD = 8, 64
    GRID = 64
    ROWS = T // GRID
    RB, CB = rpb.shape[2], rpb.shape[3]
    UNITS = 16

    IN1 = 0
    OUT1 = IN1 + 2 * D // 256
    FFN1 = OUT1 + D // 256
    FFN_PANELS = FC + len(GROUPS) * D // 256
    IN2 = FFN1 + FFN_PANELS
    MIX2 = IN2 + 9
    OUT2 = MIX2 + 2 * KC
    FFN2 = OUT2 + D // 256
    PANELS = FFN2 + FFN_PANELS

    with ExitStack() as ctx:
        def sb(name, shape, dt=F32):
            return ctx.enter_context(nc.sbuf_tensor(name, shape, dt))

        def sem(name):
            return ctx.enter_context(nc.semaphore(name))

        ps = ctx.enter_context(nc.psum_tensor("ps", [P, 8, 512], F32))
        xT = sb("xT", [P, KC * T])
        h_hi = sb("h_hi", [P, KC * T], F32R)
        h_lo = sb("h_lo", [P, KC * T], F32R)
        g_hi = sb("g_hi", [P, KC * T], F32R)
        g_lo = sb("g_lo", [P, KC * T], F32R)
        w_stage = sb("w_stage", [P, 2, 2 * HALF])
        w_hi = sb("w_hi", [P, 2, 2 * HALF], F32R)
        w_lo = sb("w_lo", [P, 2, 2 * HALF], F32R)
        rs = sb("rs", [P, T])
        rms = sb("rms", [P, T])
        sq_sum = sb("sq_sum", [P, T])
        sq = sb("sq", [P, 2, T])
        ident = sb("ident", [P, P])
        ones = sb("ones", [P, P])
        head_ones = sb("head_ones", [P, P])
        eps = sb("eps", [P, 3])
        w_pool_sb = sb("w_pool_sb", [P, 4, P])
        inv_edge = sb("inv_edge", [P, 4, 2, 8])
        mask2 = sb("mask2", [P, 2, 2 * P])
        sink = sb("sink", [P, HEADS])
        neg_sink = sb("neg_sink", [P, HEADS])
        neg_max = sb("neg_max", [P, 2, 2])
        max_raw = sb("max_raw", [P, 2, 2])
        exp_sum = sb("exp_sum", [P, 2, 2])
        exp_sink = sb("exp_sink", [P, 2, 2])
        exp_all = sb("exp_all", [P, 2, 2])
        inv_sum = sb("inv_sum", [P, 2, 2])
        edge = sb("edge", [P, 2, 2, 8])
        rms_col = sb("rms_col", [P, NT])
        rs_col = sb("rs_col", [P, NT])
        vec_rows = sb("vec_rows", [P, 3, P])
        mid = sb("mid", [P, 14400])

        vec_of = {}
        vec_loads = []
        V_ROWS = [0, 0, 0]

        def vector_rows(name, tile, src):
            vec_of[name] = sum(V_ROWS[:tile]) + V_ROWS[tile]
            vec_loads.append((tile, V_ROWS[tile], src))
            V_ROWS[tile] += src.shape[0]

        for name, a in (("norm1", norm1_g[0]), ("norm2", norm2_g[0]), ("mix", mix_norm_2[0]),
                        ("ffn", ffn_norm_2[0]), ("final", final_norm_2), ("b_in", b_in_2[0]),
                        ("pool", pool_scale[0])):
            vector_rows(name, 0, a.rearrange("(r c) -> r c", c=P))
        vector_rows("conv", 0, conv_w_2[0].rearrange("t (r c) -> (t r) c", c=P))
        vec_of["q"] = V_ROWS[0]
        vec_of["k"] = V_ROWS[0] + 1
        Q_ROW = V_ROWS[0]
        V_ROWS[0] += 2
        taps = ffn_conv_w_2[0].rearrange("t (r c) -> t r c", c=P)
        FR = 2 * FC
        vector_rows("fconv0", 1, taps[0])
        vector_rows("fconv1", 1, taps[1])
        vector_rows("fconv2", 2, taps[2])
        NV = sum(V_ROWS)
        vec = sb("vec", [P, NV])

        def col(name, i=0):
            return vec[:, bass.ds(vec_of[name] + i, 1)]

        x_in = mid[:, 0:NT * D].rearrange("p (t d) -> p t d", t=NT)
        q1 = mid[:, 0:2048].rearrange("p (a t) -> p a t", a=4)
        k1 = mid[:, 2048:4096].rearrange("p (a t) -> p a t", a=4)
        v1 = mid[:, 4096:6144].rearrange("p (j c) -> p j c", j=4)
        bias = mid[:, 6144:10240]
        p1 = mid[:, 10240:11264].rearrange("p (b s) -> p b s", b=2)
        pt1 = mid[:, 11264:12288].rearrange("p (b s) -> p b s", b=2)
        PAD = 8
        U = T + 2 * PAD
        u_pad = mid[:, 12288:12288 + 2 * U].rearrange("p (b s) -> p b s", b=2)
        win = mid[:, 12288 + 2 * U:12288 + 4 * U].rearrange("p (b s) -> p b s", b=2)
        v_t = u_pad
        BR = 256
        bias_in = mid[:, 4096:4096 + HEADS * BR].rearrange("p (h s) -> p h s", h=HEADS)
        bias_in_edge = mid[:, 12288:12288 + HEADS * BR].rearrange("p (h s) -> p h s", h=HEADS)
        q2 = mid[:, 0:2048].rearrange("p (a t) -> p a t", a=4)
        k2 = mid[:, 2048:3072].rearrange("p (a t) -> p a t", a=2)
        v2 = mid[:, 3072:3584].rearrange("p (n c) -> p n c", n=4)
        v2_t = mid[:, 3584:4096]
        p2 = mid[:, 4096:5120].rearrange("p (b s) -> p b s", b=2)
        pt2 = mid[:, 5120:6144].rearrange("p (b s) -> p b s", b=2)
        cb = mid[:, 6144:8192].rearrange("p (a t) -> p a t", a=4)
        cc = mid[:, 8192:10240].rearrange("p (a t) -> p a t", a=4)
        CZ = T + 4
        cz = mid[:, 10240:10240 + 2 * CZ].rearrange("p (b s) -> p b s", b=2)
        cy = mid[:, 11272:12296].rearrange("p (b s) -> p b s", b=2)
        cx = mid[:, 12296:13320].rearrange("p (b s) -> p b s", b=2)
        merged = mid[:, 0:4096]
        branch = mid[:, 4096:5120].rearrange("p (b s) -> p b s", b=2)
        gates = mid[:, 5120:6144].rearrange("p (b s) -> p b s", b=2)
        yT = mid[:, 0:4096]
        y_out = mid[:, 4096:8192].rearrange("p (t d) -> p t d", t=NT)
        f_in = mid[:, 8400:8400 + 4 * CZ].rearrange("p (b s) -> p b s", b=4)
        f_cv = mid[:, 10464:10464 + 4 * T].rearrange("p (b s) -> p b s", b=4)

        x_landed = [sem(f"x_landed{t}") for t in range(NT)]
        vec_landed = sem("vec_landed")
        bias_landed = sem("bias_landed")
        pool_w_landed = sem("pool_w_landed")
        w_landed = [[sem(f"w_landed{s}{m}") for m in range(2)] for s in range(2)]
        w_hi_ready = sem("w_hi_ready")
        w_lo_ready = sem("w_lo_ready")
        mm_done = sem("mm_done")
        evacuated = sem("evacuated")
        const_step = sem("const_step")
        bias_cleared = sem("bias_cleared")
        bias_step = sem("bias_step")
        bias_ready = sem("bias_ready")
        edge_ready = sem("edge_ready")
        mask_ready = sem("mask_ready")
        vec_turned = sem("vec_turned")
        vec_ready = sem("vec_ready")
        x_turned = sem("x_turned")
        x_ready = sem("x_ready")
        x_scaled = sem("x_scaled")
        x_squared = sem("x_squared")
        sum_cleared = sem("sum_cleared")
        sq_added = sem("sq_added")
        h_ready = sem("h_ready")
        norm_summed = sem("norm_summed")
        norm_rooted = sem("norm_rooted")
        rs_ready = sem("rs_ready")
        qk_squared = sem("qk_squared")
        qk_summed = sem("qk_summed")
        qk_rooted = sem("qk_rooted")
        qk_inverted = sem("qk_inverted")
        qk_ready = sem("qk_ready")
        v_turned = sem("v_turned")
        v_ready = sem("v_ready")
        scores_done = sem("scores_done")
        scores_read = sem("scores_read")
        max_read = sem("max_read")
        neg_ready = sem("neg_ready")
        exp_done = sem("exp_done")
        sink_done = sem("sink_done")
        sum_ready = sem("sum_ready")
        inv_ready = sem("inv_ready")
        probs_ready = sem("probs_ready")
        probs_turned = sem("probs_turned")
        pt_ready = sem("pt_ready")
        pv_done = sem("pv_done")
        heads_hi = sem("heads_hi")
        heads_ready = sem("heads_ready")
        pads_cleared = sem("pads_cleared")
        win_step = sem("win_step")
        pool_in = sem("pool_in")
        pool_mm = sem("pool_mm")
        pool_hi = sem("pool_hi")
        pool_ready = sem("pool_ready")
        in2_biased = sem("in2_biased")
        k2_ready = sem("k2_ready")
        cz_ready = sem("cz_ready")
        tap_act = sem("tap_act")
        tap_vec = sem("tap_vec")
        conv_hi = sem("conv_hi")
        conv_ready = sem("conv_ready")
        gate_done = sem("gate_done")
        mix_step = sem("mix_step")
        merged_hi = sem("merged_hi")
        merged_ready = sem("merged_ready")
        f_tap_act = sem("f_tap_act")
        f_tap_vec = sem("f_tap_vec")
        f_silu = sem("f_silu")
        f_prod = sem("f_prod")
        f_hi = sem("f_hi")
        f_ready = sem("f_ready")
        y_scaled = sem("y_scaled")
        waits_passed = sem("waits_passed")
        y_turned = sem("y_turned")
        y_vec = sem("y_vec")
        y_act = sem("y_act")
        out_landed = sem("out_landed")

        def chunk(t, k):
            return t[:, bass.ds(k * T, T)]

        def low_of(t):
            return t.bitcast(F32)

        def bank(n, m):
            return ps[:, 2 * (n % 2) + m, :]

        def static(n):
            return isinstance(n, int)

        def ffn_plan(base):
            plan, n = [], base
            for f0, nf in GROUPS:
                plan.append((n, n + nf, f0, nf))
                n += nf + D // 256
            return plan

        LAG = 3
        SPAN = UNITS + LAG

        def beside(first, count, units):
            steps = [(n, m, k) for n in range(first, first + count) for m in range(2)
                     for k in range(0, KC, 2)]
            cut = [len(steps) * u // units for u in range(units + 1)]
            return [steps[a:b] for a, b in zip(cut, cut[1:])] + [[] for _ in range(SPAN - units)]

        BESIDE1 = beside(IN1 + 6, 2, 12)
        BESIDE2 = beside(IN2 + 4, 5, 15)
        POOL_AT = {4: 0, 7: 1, 10: 2, 13: 3}

        def probs(p, u):
            return p[:, u % 4, :] if u % 4 < 2 else sq[:, u % 4 - 2, :]

        def unit1(u):
            return u // 2, ((3, 0) if u % 2 == 0 else (1, 2))

        def keys1(b):
            return (b - 1, b) if b else (0, 3)

        def unit2(u):
            return u // 2, ((0, 1) if u % 2 == 0 else (2, 3))

        def inner(ap):
            return ap.rearrange("p (w x) -> p w x", x=GRID)[:, :, 8:56].rearrange("p w (b c) -> p b w c", c=16)

        def border(ap):
            return ap.rearrange("p (w e c) -> p w e c", e=8, c=8)[:, :, 0:8:7, :]

        def rows_up(ap, dim):
            dims = [list(d) for d in ap.ap]
            offset = ap.offset + (ROWS - 1) * dims[dim][0]
            dims[dim][0] = -dims[dim][0]
            return bass.AP(ap.tensor, offset, dims)

        def inner_q(ap):
            return rows_up(ap[:, P:T].rearrange("p (b c w) -> p b w c", b=3, c=16), 2)

        def border_q(ap):
            return rows_up(ap[:, 0:P].rearrange("p (e c w) -> p w e c", e=2, c=8), 1)

        def by_chunk(ap):
            return ap.rearrange("p (w j c) -> p j w c", j=4, c=16)

        def twice(ap):
            return bass.AP(ap.tensor, ap.offset, [list(ap.ap[0]), [0, 2], list(ap.ap[-1])])

        block = ctx.enter_context(nc.Block())

        @block.sync
        def _(sp):
            for t in range(NT):
                sp.dma_start(x_in[:, t, :], x[0, t * P:(t + 1) * P, :]).then_inc(x_landed[t], 16)

            def load(n, s, srcs, chunks=KC):
                for m, src in enumerate(srcs):
                    if not static(n) or n >= 2:
                        sp.wait_ge(w_lo_ready, 2 * n + m - 3)
                    sp.dma_start(
                        w_stage[:, s, m * HALF:(m + 1) * HALF].rearrange("p (k c) -> p k c", c=P)[:, 0:chunks, :],
                        src.rearrange("(k p) c -> p k c", p=P)).then_inc(w_landed[s][m], 16)

            def cols(w, c):
                return w[:, bass.ds(c, P)]

            def load_pairs(n0, panels, w, c0):
                with sp.Fori(0, panels // 2) as i:
                    for j in range(2):
                        c = c0 + i * 512 + j * 256
                        load(n0 + 2 * i + j, (n0 + j) % 2, [cols(w, c), cols(w, c + P)],
                             w.shape[0] // P)

            def load_ffn(base, w_g, w_u, up0, w_d):
                for n0, nd, f0, nf in ffn_plan(base):
                    with sp.Fori(0, nf // 2) as i:
                        for j in range(2):
                            c = i * 256 + (f0 + j) * P
                            load(n0 + 2 * i + j, (n0 + j) % 2, [cols(w_g, c), cols(w_u, c + up0)])
                    load_pairs(nd, D // 256, w_d[f0 * P:(f0 + nf) * P, :], 0)

            for n in range(2):
                load(IN1 + n, n % 2, [cols(w_in[0], n * 256), cols(w_in[0], n * 256 + P)])
            load_pairs(IN1 + 2, 6, w_in[0], 512)
            load_pairs(OUT1, D // 256, w_out[0], 0)
            load_ffn(FFN1, w_gate[0], w_up[0], 0, w_down[0])
            load_pairs(IN2, 8, w_in_2[0], 0)
            load(IN2 + 8, (IN2 + 8) % 2, [cols(w_in_2[0], 2048), cols(w_in_2[0], 2048 + P)])
            with sp.Fori(0, KC) as i:
                c = i * P
                load(MIX2 + 2 * i, MIX2 % 2,
                     [cols(w_attn_branch_2[0], c), cols(w_conv_branch_2[0], c)], 4)
                load(MIX2 + 2 * i + 1, (MIX2 + 1) % 2,
                     [cols(w_in_2[0], c + 2304), cols(w_in_2[0], c + 2304 + D)])
            load_pairs(OUT2, D // 256, w_out_2[0], 0)
            load_ffn(FFN2, w_up_2[0], w_up_2[0], F, w_down_2[0])
            for t in range(NT):
                sp.wait_ge(y_vec, t + 1)
                sp.wait_ge(y_act, t + 1)
                sp.dma_start(out[0, t * P:(t + 1) * P, :], y_out[:, t, :]).then_inc(out_landed, 16)
            sp.wait_ge(out_landed, 16 * NT)

        @block.gpsimd
        def _(pool):
            def select(ap, in_, base, pattern, mult, cmp=ALU.is_ge, fill=MASKED):
                return pool.affine_select(out=ap, in_=in_, compare_op=cmp, fill=fill, base=base,
                                          pattern=pattern, channel_multiplier=mult)

            def low_part(n, s):
                for m in range(2):
                    pool.wait_ge(w_hi_ready, 2 * n + m + 1)
                    c = slice(m * HALF, (m + 1) * HALF)
                    pool.tensor_tensor(w_lo[:, s, c], w_stage[:, s, c], low_of(w_hi[:, s, c]),
                                       ALU.subtract).then_inc(w_lo_ready, 1)

            pool.memset(ident[:, :], 0.0).then_inc(const_step, 1)
            pool.wait_ge(const_step, 1)
            select(ident[:, :], ident[:, :], 0, [[-1, P]], 1, ALU.not_equal, 1.0).then_inc(const_step, 1)
            pool.memset(eps[:, 0:1], 1e-6)
            pool.memset(eps[:, 1:2], 1e-5)
            pool.memset(eps[:, 2:3], HD * 1e-6)
            pool.memset(ones[:, :], 1.0)
            pool.memset(head_ones[:, :], 0.0).then_inc(const_step, 1)
            pool.wait_ge(const_step, 3)
            pool.memset(head_ones[0:HD, 0:HD], 1.0)
            pool.memset(head_ones[HD:P, HD:P], 1.0).then_inc(const_step, 1)
            pool.wait_ge(const_step, 4)
            pool.memset(bias_in[:, :, :], 0.0)
            pool.memset(bias_in_edge[:, :, :], 0.0).then_inc(bias_cleared, 1)
            low_part(0, 0)
            low_part(1, 1)

            pool.wait_ge(bias_landed, 16 * 2 * 16)
            for h in range(HEADS):
                rows = bias_in[:, h, 0:ROWS * CB].rearrange("p (w k) -> p w k", k=CB)
                edges = bias_in_edge[:, h, 0:ROWS * CB].rearrange("p (w k) -> p w k", k=CB)[:, :, 0:16]
                o = [bias[:, (4 * h + s) * P:(4 * h + s + 1) * P].rearrange("p (w k) -> p w k", k=16)
                     for s in range(4)]
                select(o[0], rows[:, :, 0:16], ROWS - 1, [[0, ROWS], [ROWS, 16]], -1)
                select(o[1][:, :, 0:15], rows[:, :, 16:31], -ROWS, [[0, ROWS], [-ROWS, 15]], 1)
                pool.memset(o[1][:, :, 15:16], MASKED)
                select(o[2], edges, P // 2 - 1, [[0, ROWS], [0, 16]], -1)
                last = select(o[3], edges, -P // 2, [[0, ROWS], [0, 16]], 1)
            last.then_inc(bias_ready, 1)
            low_part(2, 0)
            low_part(3, 1)

            for g in range(4):
                w = 1 << g
                pool.memset(inv_edge[:, g, 0, w:8], 0.5 / w) if w < 8 else None
                pool.memset(inv_edge[:, g, 1, 0:9 - w], 0.5 / w)
                for i in range(w):
                    pool.memset(inv_edge[:, g, 0, i:i + 1], 1.0 / (w + i))
                for i in range(9 - w, 8):
                    pool.memset(inv_edge[:, g, 1, i:i + 1], 1.0 / (w + 8 - i))
            pool.memset(mask2[:, 0, 0:P], MASKED)
            pool.memset(mask2[:, 0, P:2 * P], 0.0)
            pool.memset(mask2[:, 1, :], 0.0).then_inc(edge_ready, 1)
            pool.wait_ge(edge_ready, 1)
            select(mask2[:, 1, 0:P], mask2[:, 1, 0:P], -1, [[1, P]], -1)
            select(mask2[:, 1, P:2 * P], mask2[:, 1, P:2 * P], 0, [[-1, P]], 1)
            select(mask2[:, 0, P:2 * P], mask2[:, 0, P:2 * P], 0, [[-1, P]], 1).then_inc(mask_ready, 1)

            with pool.Fori(2, PANELS // 2) as i:
                for j in range(2):
                    low_part(2 * i + j, j)
            low_part(PANELS - 1, (PANELS - 1) % 2)

        @block.scalar
        def _(act):
            for tile, r, src in vec_loads:
                act.dma_start(vec_rows[r:r + src.shape[0], tile, :], src).then_inc(vec_landed, 16)
            for i, g in enumerate((q_norm_g, k_norm_g)):
                for e in range(2):
                    act.dma_start(vec_rows[Q_ROW + i:Q_ROW + i + 1, 0, e * HD:(e + 1) * HD], g)\
                       .then_inc(vec_landed, 16)
            act.dma_start(sink[:, :], bass.AP(sinks_2.tensor, sinks_2.offset, [[0, P], [1, HEADS]]))\
               .then_inc(vec_landed, 16)
            act.wait_ge(bias_cleared, 1)
            run = (ROWS - 1) * CB + 16
            for c in range(16):
                for dst, shift, first in ((bias_in, c, 7), (bias_in_edge, 0, 15 - c)):
                    act.dma_start(dst[c * ROWS:(c + 1) * ROWS, :, shift:shift + run],
                                  bass.AP(rpb.tensor, rpb.offset + first,
                                          [[CB, ROWS], [RB * CB, HEADS], [1, run]])).then_inc(bias_landed, 16)
            act.dma_start(w_pool_sb[:, :, :], w_pool[0].rearrange("g c d -> c g d")).then_inc(pool_w_landed, 16)

            def wait_apart(signal, value):
                act.wait_ge(signal, value)
                act.sem_inc(waits_passed, 1)

            def high_part(n, s, m):
                act.wait_ge(w_landed[s][m], 8 * n - 8 * s + 16)
                if not static(n) or n >= 2:
                    act.wait_ge(mm_done, 2 * n + m - 3)
                c = slice(m * HALF, (m + 1) * HALF)
                act.activation(w_hi[:, s, c], w_stage[:, s, c], ACT.Copy).then_inc(w_hi_ready, 1)

            def ahead(n, s, blocks=(0, 1)):
                if not static(n) or n + 2 < PANELS:
                    for m in blocks:
                        high_part(n + 2, s, m)

            def norm_chunk(r, m, par, gain):
                act.activation(chunk(h_hi, m), chunk(xT, m), ACT.Copy, scale=col(gain, m)).then_inc(x_scaled, 1)
                if r or m >= 2:
                    wait_apart(sq_added, KC * r + m - 1)
                act.activation(sq[:, par, :], chunk(xT, m), ACT.Square).then_inc(x_squared, 1)

            def norm_root(r):
                act.wait_ge(norm_summed, r + 1)
                e = 0 if r < 2 else 1
                act.activation(rms[:, :], ps[:, 4, :], ACT.Sqrt, scale=1.0 / D,
                               bias=eps[:, e:e + 1]).then_inc(norm_rooted, 1)

            act.wait_ge(const_step, 3)
            act.wait_ge(vec_ready, 1)
            for m in range(KC):
                act.wait_ge(x_ready, m + 1)
                norm_chunk(0, m, m % 2, "norm1")
                if m % 2:
                    high_part(m // 4, m // 4, m // 2 % 2)

            def qk_squares(n):
                for c in (2 * n, 2 * n + 1):
                    act.wait_ge(evacuated, c + 1)
                    if c >= 2:
                        act.wait_ge(qk_summed, c - 1)
                    act.activation(p1[:, c % 2, :], (q1 if c < 4 else k1)[:, c % 4, :],
                                   ACT.Square).then_inc(qk_squared, 1)

            def qk_roots(n):
                for c in (2 * n, 2 * n + 1):
                    act.wait_ge(qk_summed, c + 1)
                    if c >= 2:
                        act.wait_ge(qk_ready, c - 1)
                    act.activation(pt1[:, c % 2, :], ps[:, 5 + c % 2, :], ACT.Sqrt,
                                   scale=1.0 if c < 4 else 1.0 / HD,
                                   bias=eps[:, 2:3] if c < 4 else eps[:, 0:1]).then_inc(qk_rooted, 1)

            norm_root(0)
            ahead(0, 0)
            qk_squares(0)
            for n in range(1, 4):
                ahead(n, n % 2)
                qk_squares(n)
                qk_roots(n - 1)
            qk_roots(3)
            ahead(4, 0)
            ahead(5, 1)

            def exps(u, p, ready, count):
                act.wait_ge(ready, count)
                for i in range(2):
                    q = probs(p, u)[:, i * 256:(i + 1) * 256]
                    act.activation(q, q, ACT.Exp, bias=neg_max[:, u % 2, i:i + 1],
                                   accum_out=exp_sum[:, u % 2, i:i + 1]).then_inc(exp_done, 1)

            def copy_pt(u, pt):
                act.wait_ge(probs_turned, u + 1)
                if u >= 2:
                    act.wait_ge(pv_done, u - 1)
                act.activation(pt[:, u % 2, :], ps[:, 6, :], ACT.Copy).then_inc(pt_ready, 1)

            for u in range(SPAN):
                if u < UNITS:
                    exps(u, p1, max_read, u + 1)
                if 2 <= u < UNITS + 2:
                    copy_pt(u - 2, pt1)
                if u >= 6 and u % 4 == 2:
                    a = (u - 6) // 4
                    act.wait_ge(pv_done, 4 * a + 4)
                    act.activation(inner(chunk(g_hi, a)), inner_q(ps[:, 7, :]), ACT.Copy)
                    act.activation(border(chunk(g_hi, a)), border_q(ps[:, 7, :]), ACT.Copy).then_inc(heads_hi, 1)
                for n, m, k in BESIDE1[u]:
                    if k == KC - 2:
                        ahead(n, n % 2, [m])
                if u in POOL_AT:
                    g = POOL_AT[u]
                    act.wait_ge(pool_mm, g + 1)
                    act.activation(chunk(g_hi, 4 + g), ps[:, g, :], ACT.Copy, scale=col("pool", g))\
                       .then_inc(pool_hi, 1)

            def update_norm(n0, r, gain):
                with act.Fori(0, 2) as i:
                    for j in range(2):
                        n = n0 + 2 * i + j
                        for e in range(2):
                            m = 4 * i + 2 * j + e
                            if gain != "final":
                                ahead(n, (n0 + j) % 2, [e])
                            wait_apart(evacuated, 2 * n + e + 1)
                            if gain == "final":
                                act.activation(chunk(yT, m), chunk(xT, m), ACT.Copy, scale=col(gain, m))\
                                   .then_inc(y_scaled, 1)
                                wait_apart(sq_added, KC * r + m - 1)
                                act.activation(sq[:, e, :], chunk(xT, m), ACT.Square).then_inc(x_squared, 1)
                            else:
                                norm_chunk(r, m, e, gain)

            def ffn(base, r, second):
                done = FC if second else 0
                for gi, (n0, nd, f0, nf) in enumerate(ffn_plan(base)):
                    if gi == 0:
                        norm_root(r)
                    with act.Fori(0, nf // 2) as i:
                        for j in range(2):
                            n = n0 + 2 * i + j
                            f = done + f0 + j + 2 * i
                            gate, up = (f_cv if second else f_in)[:, j, 0:T], (f_cv if second else f_in)[:, 2 + j, 0:T]
                            ahead(n, (n0 + j) % 2)
                            wait_apart(evacuated, 2 * n + 1)
                            if second:
                                c = f0 + j + 2 * i
                                act.activation(gate, f_in[:, j, 2:2 + T], ACT.Copy,
                                               scale=col("fconv2", c)).then_inc(f_tap_act, 1)
                                wait_apart(evacuated, 2 * n + 2)
                                act.activation(up, f_in[:, 2 + j, 2:2 + T], ACT.Copy,
                                               scale=col("fconv2", c + FC)).then_inc(f_tap_act, 1)
                                act.wait_ge(f_tap_vec, 4 * (f - FC) + 3)
                            act.activation(gate, gate, ACT.Silu).then_inc(f_silu, 1)
                            wait_apart(f_prod, f + 1)
                            act.activation(chunk(g_hi, 2 * i + j), up, ACT.Copy).then_inc(f_hi, 1)
                    if gi < len(GROUPS) - 1:
                        with act.Fori(0, 2) as i:
                            for j in range(2):
                                ahead(nd + 2 * i + j, (nd + j) % 2)
                    elif not second:
                        update_norm(nd, 2, "mix")
                    else:
                        ahead(nd, nd % 2)
                        ahead(nd + 1, (nd + 1) % 2)
                        update_norm(nd, 4, "final")

            update_norm(OUT1, 1, "norm2")
            ffn(FFN1, 1, False)

            def add_bias(ap, n, m, b):
                act.wait_ge(evacuated, 2 * n + m + 1)
                act.activation(ap, ap, ACT.Identity, bias=col("b_in", b)).then_inc(in2_biased, 1)

            norm_root(2)
            for n in range(3):
                ahead(IN2 + n, (IN2 + n) % 2)
                for m in range(2):
                    j = 2 * n + m
                    add_bias(q2[:, j, :] if j < 4 else (k2[:, 0, :] if j == 4 else v2_t), IN2 + n, m, j)
            ahead(IN2 + 3, (IN2 + 3) % 2)

            for u in range(SPAN):
                g = UNITS + u
                if u < UNITS:
                    exps(g, p2, neg_ready, u + 1)
                    act.activation(exp_sink[:, g % 2, :], neg_max[:, g % 2, :], ACT.Exp,
                                   bias=sink[:, u // 2:u // 2 + 1]).then_inc(sink_done, 1)
                if 2 <= u < UNITS + 2:
                    copy_pt(g - 2, pt2)
                if u >= 6 and u % 4 == 2:
                    a = (u - 6) // 4
                    act.wait_ge(pv_done, UNITS + 4 * a + 4)
                    act.activation(chunk(g_hi, a), ps[:, 7, :], ACT.Copy).then_inc(heads_hi, 1)
                for n, m, k in BESIDE2[u]:
                    if k == KC - 2:
                        ahead(n, n % 2, [m])
                        if n >= IN2 + 7:
                            c = 2 * (n - IN2 - 7) + m
                            add_bias(cx[:, m, :], n, m, 14 + c)
                            act.wait_ge(cz_ready, c + 1)
                            act.activation(cy[:, m, :], cz[:, m, 2:2 + T], ACT.Copy,
                                           scale=col("conv", 8 + c)).then_inc(tap_act, 1)
                            act.wait_ge(tap_vec, 3 * c + 3)
                            act.activation(chunk(g_hi, 4 + c), cy[:, m, :], ACT.Copy).then_inc(conv_hi, 1)

            def gate_pair(m):
                for e in range(2):
                    wait_apart(evacuated, 2 * MIX2 + 4 * m + 3 + e)
                    act.activation(gates[:, e, :], gates[:, e, :], ACT.Sigmoid,
                                   bias=col("b_in", 18 + KC * e + m)).then_inc(gate_done, 1)

            def merged_high(m):
                act.wait_ge(mix_step, 3 * m + 3)
                act.activation(chunk(g_hi, m), chunk(merged, m), ACT.Copy).then_inc(merged_hi, 1)

            with act.Fori(0, KC - 1) as i:
                ahead(MIX2 + 2 * i, MIX2 % 2)
                gate_pair(i)
                ahead(MIX2 + 1 + 2 * i, (MIX2 + 1) % 2)
            ahead(OUT2 - 2, OUT2 % 2)
            for m in range(KC - 1):
                merged_high(m)
            gate_pair(KC - 1)
            ahead(OUT2 - 1, (OUT2 - 1) % 2)
            merged_high(KC - 1)

            update_norm(OUT2, 3, "ffn")
            ffn(FFN2, 3, True)
            act.wait_ge(norm_summed, 5)
            act.activation(rms_col[:, :], ps[:, 6, 0:NT], ACT.Sqrt, scale=1.0 / D, bias=eps[:, 1:2])\
               .then_inc(norm_rooted, 1)
            act.wait_ge(rs_ready, 5)
            for t in range(NT):
                act.wait_ge(y_turned, t + 1)
                act.activation(y_out[:, t, 0:512], ps[:, 2 * (t % 3), :], ACT.Copy, scale=rs_col[:, t:t + 1])\
                   .then_inc(y_act, 1)

        @block.vector
        def _(dve):
            def take_in(n, m, par, out):
                dve.wait_ge(mm_done, 2 * n + m + 1)
                dve.tensor_tensor(out, bank(par, m), rs[:, :], ALU.mult).then_inc(evacuated, 1)

            def add_squares(r, m, par):
                dve.wait_ge(x_squared, KC * r + m + 1)
                if not static(m) or m:
                    dve.wait_ge(sq_added, KC * r + m)
                dve.wait_ge(sum_cleared, r + 1)
                dve.tensor_tensor(sq_sum[:, :], sq_sum[:, :], sq[:, par, :], ALU.add).then_inc(sq_added, 1)

            def norm_low(r, m, par, gain):
                dve.wait_ge(x_scaled, KC * r + m + 1)
                dve.scalar_tensor_tensor(chunk(h_lo, m), chunk(xT, m), col(gain, m),
                                         low_of(chunk(h_hi, m)), ALU.mult, ALU.subtract)\
                   .then_inc(h_ready, 1)
                add_squares(r, m, par)

            def norm_factor(r):
                dve.wait_ge(norm_rooted, r + 1)
                dve.reciprocal(rs[:, :], rms[:, :]).then_inc(rs_ready, 1)
                dve.memset(sq_sum[:, :], 0.0).then_inc(sum_cleared, 1)
                dve.wait_ge(rs_ready, r + 1)

            dve.memset(sq_sum[:, :], 0.0).then_inc(sum_cleared, 1)
            dve.wait_ge(vec_turned, 1)
            dve.tensor_copy(vec[:, :], ps[:, 5, 0:NV])
            dve.tensor_scalar(neg_sink[:, :], sink[:, :], -1.0, None, ALU.mult).then_inc(vec_ready, 1)
            dve.wait_ge(vec_ready, 1)
            for m in range(KC):
                dve.wait_ge(x_turned, m + 1)
                dve.tensor_copy(chunk(xT, m), ps[:, m % 4, :]).then_inc(x_ready, 1)
                if m:
                    norm_low(0, m - 1, (m - 1) % 2, "norm1")
            norm_low(0, KC - 1, 1, "norm1")
            norm_factor(0)

            def qk_take(n):
                for m in range(2):
                    c = 2 * n + m
                    if c >= 4:
                        take_in(n, m, n, k1[:, c - 4, :])
                        continue
                    dve.wait_ge(mm_done, c + 1)
                    dve.tensor_tensor(inner_q(q1[:, c, :]), inner(bank(n, m)), inner(rs[:, :]), ALU.mult)
                    dve.tensor_tensor(border_q(q1[:, c, :]), border(bank(n, m)), border(rs[:, :]),
                                      ALU.mult).then_inc(evacuated, 1)

            def qk_norm(n):
                for c in (2 * n, 2 * n + 1):
                    dve.wait_ge(qk_rooted, c + 1)
                    dve.reciprocal(pt1[:, c % 2, :], pt1[:, c % 2, :]).then_inc(qk_inverted, 1)
                    dve.wait_ge(qk_inverted, c + 1)
                    x_ = (q1 if c < 4 else k1)[:, c % 4, :]
                    dve.scalar_tensor_tensor(x_, x_, col("q" if c < 4 else "k"), pt1[:, c % 2, :],
                                             ALU.mult, ALU.mult).then_inc(qk_ready, 1)

            def v_take(n):
                for m in range(2):
                    a = 2 * (n - 4) + m
                    if a >= 2:
                        dve.wait_ge(v_turned, a - 1)
                    dve.wait_ge(mm_done, 2 * n + m + 1)
                    dve.tensor_tensor(v_t[:, m, 0:T].rearrange("p (j w c) -> p j w c", j=4, c=16),
                                      by_chunk(bank(n, m)), by_chunk(rs[:, :]), ALU.mult).then_inc(evacuated, 1)

            def v_copy(a):
                dve.wait_ge(v_turned, a + 1)
                dve.tensor_copy(v1[:, :, a * P:(a + 1) * P],
                                ps[:, 6 + a % 2, :].rearrange("p (j c) -> p j c", j=4)).then_inc(v_ready, 1)

            def normalise(u, p):
                i = u % 2
                dve.wait_ge(exp_done, 2 * u + 2)
                total = exp_sum[:, i, :]
                if u >= UNITS:
                    dve.wait_ge(sink_done, u - UNITS + 1)
                    dve.tensor_tensor(exp_all[:, i, :], total, exp_sink[:, i, :], ALU.add).then_inc(sum_ready, 1)
                    dve.wait_ge(sum_ready, u - UNITS + 1)
                    total = exp_all[:, i, :]
                dve.reciprocal(inv_sum[:, i, :], total).then_inc(inv_ready, 1)
                dve.wait_ge(inv_ready, u + 1)
                for b in range(2):
                    q = probs(p, u)[:, b * 256:(b + 1) * 256]
                    ins = dve.tensor_scalar(q, q, inv_sum[:, i, b:b + 1], None, ALU.mult)
                ins.then_inc(probs_ready, 1)

            def unit_max(u, p, out, signal):
                dve.wait_ge(scores_read, u + 1)
                dve.reduce_max(out[:, u % 2, :], probs(p, u).rearrange("p (b k) -> p b k", b=2),
                               AX_X, negate=True).then_inc(signal, 1)

            qk_take(0)
            for n in range(1, 4):
                qk_take(n)
                qk_norm(n - 1)
            dve.wait_ge(bias_ready, 1)
            v_take(4)
            qk_norm(3)
            v_copy(0)
            v_copy(1)
            v_take(5)

            def pool_group(n, m):
                g = 2 * (n - 6) + m
                if g >= 2:
                    dve.wait_ge(pool_mm, g - 1)
                body = u_pad[:, m, PAD:PAD + T]
                take_in(n, m, n, body)
                dve.wait_ge(evacuated, 2 * n + m + 1)
                src, n_in = u_pad[:, m, :], U
                for k in range(g + 1):
                    d = 1 << k
                    o = win[:, k % 2, 0:n_in - d]
                    dve.tensor_tensor(o, src[:, 0:n_in - d], src[:, d:n_in], ALU.add).then_inc(win_step, 1)
                    dve.wait_ge(win_step, steps_before(g) + k + 1)
                    src, n_in = win[:, k % 2, :], n_in - d
                w = 1 << g
                sums = src[:, PAD - w:PAD - w + T]

                def ends(ap):
                    return ap.rearrange("p (b x) -> p b x", x=8)[:, 0:64:63, :]

                dve.tensor_tensor(edge[:, m, :, :], ends(sums), inv_edge[:, g, :, :], ALU.mult).then_inc(win_step, 1)
                dve.wait_ge(win_step, steps_before(g) + g + 2)
                dve.tensor_tensor(edge[:, m, :, :], edge[:, m, :, :], ends(body), ALU.subtract).then_inc(win_step, 1)
                dve.wait_ge(win_step, steps_before(g) + g + 3)
                dve.scalar_tensor_tensor(body, sums, 0.5 / w, body, ALU.mult, ALU.subtract).then_inc(win_step, 1)
                dve.wait_ge(win_step, steps_before(g) + g + 4)
                dve.tensor_copy(ends(body), edge[:, m, :, :]).then_inc(pool_in, 1)

            def steps_before(g):
                return sum(4 + i for i in range(g))

            for u in range(SPAN):
                if u < UNITS:
                    h, bs = unit1(u)
                    dve.wait_ge(scores_done, u + 1)
                    if u >= 4:
                        dve.wait_ge(probs_turned, u - 3)
                    tab = bias[:, h * 512:h * 512 + 256]
                    if bs == (3, 0):
                        dve.tensor_tensor(probs(p1, u), ps[:, 4 + u % 2, :], bias[:, h * 512:(h + 1) * 512],
                                          ALU.add).then_inc(scores_read, 1)
                    else:
                        dve.tensor_tensor(probs(p1, u).rearrange("p (b k) -> p b k", b=2),
                                          ps[:, 4 + u % 2, :].rearrange("p (b k) -> p b k", b=2), twice(tab),
                                          ALU.add).then_inc(scores_read, 1)
                    unit_max(u, p1, neg_max, max_read)
                if u == 0:
                    v_copy(2)
                    v_copy(3)
                    dve.memset(u_pad[:, :, 0:PAD], 0.0)
                    dve.memset(u_pad[:, :, PAD + T:U], 0.0).then_inc(pads_cleared, 1)
                    dve.wait_ge(pads_cleared, 1)
                    dve.wait_ge(edge_ready, 1)
                if 1 <= u <= UNITS:
                    normalise(u - 1, p1)
                if u >= 6 and u % 4 == 2:
                    a = (u - 6) // 4
                    dve.wait_ge(heads_hi, a + 1)
                    dve.tensor_tensor(inner(chunk(g_lo, a)), inner_q(ps[:, 7, :]),
                                      inner(low_of(chunk(g_hi, a))), ALU.subtract)
                    dve.tensor_tensor(border(chunk(g_lo, a)), border_q(ps[:, 7, :]),
                                      border(low_of(chunk(g_hi, a))), ALU.subtract).then_inc(heads_ready, 1)
                for n, m, k in BESIDE1[u]:
                    if k == KC - 2:
                        pool_group(n, m)
                if u in POOL_AT:
                    g = POOL_AT[u]
                    dve.wait_ge(pool_hi, g + 1)
                    dve.scalar_tensor_tensor(chunk(g_lo, 4 + g), ps[:, g, :], col("pool", g),
                                             low_of(chunk(g_hi, 4 + g)), ALU.mult, ALU.subtract)\
                       .then_inc(pool_ready, 1)

            def update(n, e, par, m):
                dve.wait_ge(mm_done, 2 * n + e + 1)
                dve.tensor_tensor(chunk(xT, m), chunk(xT, m), bank(par, e), ALU.add).then_inc(evacuated, 1)

            def update_norm(n0, r, gain):
                with dve.Fori(0, 2) as i:
                    for j in range(2):
                        n = n0 + 2 * i + j
                        for e in range(2):
                            update(n, e, n0 + j, 4 * i + 2 * j + e)
                        for e in range(2):
                            dve.wait_ge(evacuated, 2 * n + e + 1)
                            if gain == "final":
                                add_squares(r, 4 * i + 2 * j + e, e)
                            else:
                                norm_low(r, 4 * i + 2 * j + e, e, gain)

            def ffn(base, r, second):
                done = FC if second else 0
                norm_factor(r)
                for gi, (n0, nd, f0, nf) in enumerate(ffn_plan(base)):
                    with dve.Fori(0, nf // 2) as i:
                        for j in range(2):
                            n = n0 + 2 * i + j
                            f = done + f0 + j + 2 * i
                            off = 2 if second else 0
                            for e in range(2):
                                take_in(n, e, n0 + j, f_in[:, 2 * e + j, off:off + T])
                            if second:
                                c = f0 + j + 2 * i
                                for tap in range(2):
                                    for e in range(2):
                                        o = f_cv[:, 2 * e + j, :]
                                        if tap:
                                            dve.wait_ge(f_tap_vec, 4 * (f - FC) + e + 1)
                                        else:
                                            dve.wait_ge(evacuated, 2 * n + e + 1)
                                            dve.wait_ge(f_tap_act, 2 * (f - FC) + e + 1)
                                        dve.scalar_tensor_tensor(
                                            o, f_in[:, 2 * e + j, 1 - tap:1 - tap + T],
                                            col(f"fconv{1 - tap}", c + FC * e), o, ALU.mult, ALU.add)\
                                           .then_inc(f_tap_vec, 1)
                                dve.wait_ge(f_tap_vec, 4 * (f - FC) + 4)
                            else:
                                dve.wait_ge(evacuated, 2 * n + 2)
                            t = f_cv if second else f_in
                            gate, up = t[:, j, 0:T], t[:, 2 + j, 0:T]
                            dve.wait_ge(f_silu, f + 1)
                            dve.tensor_tensor(up, gate, up, ALU.mult).then_inc(f_prod, 1)
                            dve.wait_ge(f_hi, f + 1)
                            dve.tensor_tensor(chunk(g_lo, 2 * i + j), up, low_of(chunk(g_hi, 2 * i + j)),
                                              ALU.subtract).then_inc(f_ready, 1)
                    if gi < len(GROUPS) - 1:
                        with dve.Fori(0, 2) as i:
                            for j in range(2):
                                for e in range(2):
                                    update(nd + 2 * i + j, e, nd + j, 4 * i + 2 * j + e)
                    else:
                        update_norm(nd, 4 if second else 2, "final" if second else "mix")

            update_norm(OUT1, 1, "norm2")
            ffn(FFN1, 1, False)

            norm_factor(2)
            dve.memset(cz[:, :, 0:2], 0.0).then_inc(pads_cleared, 1)
            for n in range(3):
                for m in range(2):
                    j = 2 * n + m
                    take_in(IN2 + n, m, IN2 + n, q2[:, j, :] if j < 4 else (k2[:, 0, :] if j == 4 else v2_t))
            dve.wait_ge(in2_biased, 5)
            dve.tensor_copy(k2[0:HD, 1, :], k2[HD:P, 0, :])
            dve.tensor_copy(k2[HD:P, 1, :], k2[0:HD, 0, :]).then_inc(k2_ready, 1)
            for m in range(2):
                take_in(IN2 + 3, m, IN2 + 3, cb[:, m, :])
            dve.wait_ge(v_turned, 5)
            dve.tensor_copy(v2[:, :, :], ps[:, 6, :].rearrange("p (n c) -> p n c", n=4)).then_inc(v_ready, 1)
            dve.wait_ge(pads_cleared, 2)
            dve.wait_ge(mask_ready, 1)

            def conv_chunk(n, m):
                c = 2 * (n - IN2 - 7) + m
                y = cy[:, m, :]
                dve.wait_ge(in2_biased, 6 + c + 1)
                dve.scalar_tensor_tensor(cz[:, m, 2:2 + T], cc[:, c, :], col("b_in", 10 + c), cx[:, m, :],
                                         ALU.add, ALU.mult).then_inc(cz_ready, 1)
                dve.wait_ge(cz_ready, c + 1)
                dve.wait_ge(tap_act, c + 1)
                for tap in range(2):
                    dve.scalar_tensor_tensor(y, cz[:, m, 1 - tap:1 - tap + T], col("conv", 4 * (1 - tap) + c), y,
                                             ALU.mult, ALU.add).then_inc(tap_vec, 1)
                    dve.wait_ge(tap_vec, 3 * c + tap + 1)
                dve.scalar_tensor_tensor(y, cb[:, c, :], col("b_in", 6 + c), y, ALU.add, ALU.mult)\
                   .then_inc(tap_vec, 1)
                dve.wait_ge(conv_hi, c + 1)
                dve.wait_ge(tap_vec, 3 * c + 3)
                dve.tensor_tensor(chunk(g_lo, 4 + c), y, low_of(chunk(g_hi, 4 + c)), ALU.subtract)\
                   .then_inc(conv_ready, 1)

            for u in range(SPAN):
                g = UNITS + u
                if u < UNITS:
                    h, bs = unit2(u)
                    dve.wait_ge(scores_done, g + 1)
                    dve.wait_ge(probs_turned, g - 3)
                    m = mask2[:, :, :] if bs == (0, 1) else twice(mask2[:, 1, :])
                    dve.scalar_tensor_tensor(probs(p2, g).rearrange("p (b k) -> p b k", b=2),
                                             ps[:, 4 + g % 2, :].rearrange("p (b k) -> p b k", b=2),
                                             HD ** -0.5, m, ALU.mult, ALU.add).then_inc(scores_read, 1)
                    unit_max(g, p2, max_raw, max_read)
                    dve.wait_ge(max_read, g + 1)
                    dve.tensor_scalar(neg_max[:, g % 2, :], max_raw[:, g % 2, :], neg_sink[:, h:h + 1], None,
                                      ALU.min).then_inc(neg_ready, 1)
                if 1 <= u <= UNITS:
                    normalise(g - 1, p2)
                if u >= 6 and u % 4 == 2:
                    a = (u - 6) // 4
                    dve.wait_ge(heads_hi, 4 + a + 1)
                    dve.tensor_tensor(chunk(g_lo, a), ps[:, 7, :], low_of(chunk(g_hi, a)), ALU.subtract)\
                       .then_inc(heads_ready, 1)
                for n, m, k in BESIDE2[u]:
                    if k == KC - 2:
                        j = 2 * (n - IN2) + m
                        take_in(n, m, n, cb[:, j - 6, :] if j < 10 else (cc[:, j - 10, :] if j < 14 else cx[:, m, :]))
                        if n >= IN2 + 7:
                            conv_chunk(n, m)

            def take_branches(m):
                n = MIX2 + 2 * m
                for e in range(2):
                    dve.wait_ge(mm_done, 2 * n + e + 1)
                    dve.tensor_copy(branch[:, e, :], bank(MIX2, e)).then_inc(evacuated, 1)

            def merge(m):
                n = MIX2 + 2 * m + 1
                for e in range(2):
                    take_in(n, e, MIX2 + 1, gates[:, e, :])
                for e in range(2):
                    dve.wait_ge(gate_done, 2 * m + e + 1)
                    dve.tensor_tensor(branch[:, e, :], branch[:, e, :], gates[:, e, :], ALU.mult).then_inc(mix_step, 1)
                dve.wait_ge(mix_step, 3 * m + 2)
                dve.tensor_tensor(chunk(merged, m), branch[:, 0, :], branch[:, 1, :], ALU.add).then_inc(mix_step, 1)
                dve.wait_ge(mix_step, 3 * m + 3)

            def merged_low(m):
                dve.wait_ge(merged_hi, m + 1)
                dve.tensor_tensor(chunk(g_lo, m), chunk(merged, m), low_of(chunk(g_hi, m)), ALU.subtract)\
                   .then_inc(merged_ready, 1)

            with dve.Fori(0, KC - 1) as i:
                take_branches(i)
                merge(i)
            take_branches(KC - 1)
            for m in range(KC - 1):
                merged_low(m)
            merge(KC - 1)
            merged_low(KC - 1)

            update_norm(OUT2, 3, "ffn")
            dve.memset(f_in[:, :, 0:2], 0.0).then_inc(pads_cleared, 1)
            dve.wait_ge(pads_cleared, 3)
            ffn(FFN2, 3, True)
            dve.wait_ge(norm_rooted, 5)
            dve.reciprocal(rs_col[:, :], rms_col[:, :]).then_inc(rs_ready, 1)
            dve.wait_ge(rs_ready, 5)
            for t in range(NT):
                dve.wait_ge(y_turned, t + 1)
                dve.tensor_scalar(y_out[:, t, 512:1024], ps[:, 2 * (t % 3) + 1, :], rs_col[:, t:t + 1], None,
                                  ALU.mult).then_inc(y_vec, 1)

        @block.tensor
        def _(pe):
            def step(par, blocks, k, operands, first, last):
                for m in blocks:
                    x_hi, x_lo = operands(m, k)
                    w = slice(m * HALF + k * P, m * HALF + (k + 1) * P)
                    wh, wl = w_hi[:, par, w], w_lo[:, par, w]
                    for i, (a, b) in enumerate(((wh, x_hi), (wh, x_lo), (wl, x_hi))):
                        ins = pe.matmul(bank(par, m), a, b, start=first and i == 0, stop=last and i == 2)
                    if last:
                        ins.then_inc(mm_done, 1)

            def open_block(n, m):
                pe.wait_ge(w_lo_ready, 2 * n + m + 1)
                if not static(n) or n >= 2:
                    pe.wait_ge(evacuated, 2 * n + m - 3)

            def of(hi, lo):
                return lambda m, k: (hi[:, k * T:(k + 1) * T], lo[:, k * T:(k + 1) * T])

            H, G = of(h_hi, h_lo), of(g_hi, g_lo)

            def panel(n, par, operands, ready=None, base=0, order=range(KC)):
                order = list(order)
                for blocks in ([(0, 1)] if ready is not None else [(0,), (1,)]):
                    for m in blocks:
                        open_block(n, m)
                    for a, k in enumerate(order):
                        if ready is not None:
                            pe.wait_ge(ready, base + k + 1)
                        step(par % 2, blocks, k, operands, a == 0, a == len(order) - 1)

            def norm_sum(r):
                pe.wait_ge(sq_added, KC * (r + 1))
                pe.matmul(ps[:, 4, :], ones[:, :], sq_sum[:, :], start=True, stop=True).then_inc(norm_summed, 1)

            pe.wait_ge(const_step, 2)
            pe.wait_ge(vec_landed, 16 * (len(vec_loads) + 5))
            at = 0
            for tile, rows in enumerate(V_ROWS):
                ins = pe.transpose(ps[:, 5, at:at + rows], vec_rows[0:rows, tile, :], ident[0:rows, 0:rows])
                at += rows
            ins.then_inc(vec_turned, 1)
            for m in range(KC):
                if m >= 4:
                    pe.wait_ge(x_ready, m - 3)
                for t in range(NT):
                    if m == 0:
                        pe.wait_ge(x_landed[t], 16)
                    ins = pe.transpose(ps[:, m % 4, t * P:(t + 1) * P], x_in[:, t, m * P:(m + 1) * P], ident[:, :])
                ins.then_inc(x_turned, 1)

            def qk_sum(n):
                for c in (2 * n, 2 * n + 1):
                    pe.wait_ge(qk_squared, c + 1)
                    if c >= 2:
                        pe.wait_ge(qk_rooted, c - 1)
                    pe.matmul(ps[:, 5 + c % 2, :], head_ones[:, :], p1[:, c % 2, :], start=True, stop=True)\
                      .then_inc(qk_summed, 1)

            def turn_v(a):
                pe.wait_ge(evacuated, 2 * (4 + a // 2) + a % 2 + 1)
                if a == 0:
                    pe.wait_ge(qk_rooted, 8)
                if a >= 2:
                    pe.wait_ge(v_ready, a - 1)
                for j in range(4):
                    ins = pe.transpose(ps[:, 6 + a % 2, j * P:(j + 1) * P], v_t[:, a % 2, j * P:(j + 1) * P], ident[:, :])
                ins.then_inc(v_turned, 1)

            pe.wait_ge(x_ready, KC)
            panel(0, 0, H, h_ready)
            norm_sum(0)
            panel(1, 1, H)
            pe.wait_ge(const_step, 4)
            for n in range(1, 4):
                qk_sum(n - 1)
                panel(n + 1, n + 1, H)
            qk_sum(3)
            for m in range(2):
                open_block(5, m)
                for k in range(KC):
                    step(1, [m], k, H, k == 0, k == KC - 1)
                    if (m, k) == (1, 0):
                        turn_v(0)
                        turn_v(1)

            def turn_probs(u, p):
                pe.wait_ge(probs_ready, u + 1)
                if u:
                    pe.wait_ge(pt_ready, u)
                for j in range(4):
                    ins = pe.transpose(ps[:, 6, j * P:(j + 1) * P], probs(p, u)[:, j * P:(j + 1) * P], ident[:, :])
                ins.then_inc(probs_turned, 1)

            def values(u, h, bs, pt, value, keys):
                pe.wait_ge(pt_ready, u + 1)
                if u % 4 == 0 and u:
                    pe.wait_ge(heads_ready, u // 4)
                rows = slice(HD * (h % 2), HD * (h % 2) + HD)
                for i, b in enumerate(bs):
                    seen = [(s, j) for s, j in enumerate(keys(b)) if j >= 0]
                    for s, j in seen:
                        ins = pe.matmul(ps[rows, 7, b * P:(b + 1) * P], value(h, j),
                                        pt[:, u % 2, (2 * i + s) * P:(2 * i + s + 1) * P],
                                        start=(s, j) == seen[0], stop=(s, j) == seen[-1])
                ins.then_inc(pv_done, 1)

            def beside_unit(steps):
                for n, m, k in steps:
                    if k == 0:
                        open_block(n, m)
                    for kk in (k, k + 1):
                        step(n % 2, [m], kk, H, kk == 0, kk == KC - 1)

            pe.wait_ge(qk_ready, 8)
            for u in range(SPAN):
                if u < UNITS:
                    h, bs = unit1(u)
                    if u >= 2:
                        pe.wait_ge(scores_read, u - 1)
                    r = slice(HD * (h % 2), HD * (h % 2) + HD)
                    for i, b in enumerate(bs):
                        keys = by_chunk(k1[r, h // 2, :])
                        keys = keys[:, b - 1:b + 1] if b else keys[:, 0:4:3]
                        ins = pe.matmul(ps[:, 4 + u % 2, i * 256:(i + 1) * 256],
                                        q1[r, h // 2, b * P:(b + 1) * P], keys, start=True, stop=True)
                    ins.then_inc(scores_done, 1)
                beside_unit(BESIDE1[u])
                if u == 0:
                    turn_v(2)
                    turn_v(3)
                    pe.wait_ge(pool_w_landed, 16)
                if u in POOL_AT:
                    g = POOL_AT[u]
                    pe.wait_ge(pool_in, g + 1)
                    pe.matmul(ps[:, g, :], w_pool_sb[:, g, :], u_pad[:, g % 2, PAD:PAD + T], start=True,
                              stop=True).then_inc(pool_mm, 1)
                if 2 <= u < UNITS + 2:
                    if u == 2:
                        pe.wait_ge(v_ready, 4)
                    turn_probs(u - 2, p1)
                if u >= LAG:
                    values(u - LAG, *unit1(u - LAG), pt1, lambda h, j: v1[:, j, h * HD:(h + 1) * HD], keys1)

            def panels(n0, pairs, operands, order=None, first=0):
                order = list(order or range(KC))
                with pe.Fori(first, pairs) as i:
                    for j in range(2):
                        panel(n0 + 2 * i + j, n0 + j, operands, order=order)

            pe.wait_ge(pool_ready, 4)
            for m in range(2):
                open_block(OUT1, m)
            for a, k in enumerate([4, 5, 6, 7, 0, 1, 2, 3]):
                if k == 0:
                    pe.wait_ge(heads_ready, 3)
                if k == 3:
                    pe.wait_ge(heads_ready, 4)
                step(0, (0, 1), k, G, a == 0, a == KC - 1)
            panel(OUT1 + 1, 1, G)
            panels(OUT1, 2, G, first=1)

            def ffn(base, r, done):
                for gi, (n0, nd, f0, nf) in enumerate(ffn_plan(base)):
                    if gi == 0:
                        panel(n0, n0, H, h_ready, KC * r)
                        norm_sum(r)
                        panel(n0 + 1, n0 + 1, H)
                    panels(n0, nf // 2, H, first=0 if gi else 1)
                    panel(nd, nd, G, f_ready, done + f0, range(nf))
                    panel(nd + 1, nd + 1, G, order=range(nf))
                    panels(nd, 2, G, range(nf), first=1)

            ffn(FFN1, 1, 0)

            panel(IN2, IN2, H, h_ready, 2 * KC)
            norm_sum(2)
            panel(IN2 + 1, IN2 + 1, H)
            panel(IN2 + 2, IN2 + 2, H)
            for m in range(2):
                open_block(IN2 + 3, m)
                for k in range(KC):
                    step((IN2 + 3) % 2, [m], k, H, k == 0, k == KC - 1)
            pe.wait_ge(in2_biased, 6)
            for j in range(4):
                ins = pe.transpose(ps[:, 6, j * P:(j + 1) * P], v2_t[:, j * P:(j + 1) * P], ident[:, :])
            ins.then_inc(v_turned, 1)
            pe.wait_ge(k2_ready, 1)
            for u in range(SPAN):
                g = UNITS + u
                if u < UNITS:
                    h, bs = unit2(u)
                    pe.wait_ge(scores_read, g - 1)
                    r = slice(HD * (h % 2), HD * (h % 2) + HD)
                    keys = k2[r, 0 if h // 4 == h % 2 else 1, :]
                    for i, b in enumerate(bs):
                        kk = keys[:, (b - 1) * P:(b + 1) * P] if b else twice(keys[:, 0:P])
                        ins = pe.matmul(ps[:, 4 + g % 2, i * 256:(i + 1) * 256],
                                        q2[r, h // 2, b * P:(b + 1) * P], kk, start=True, stop=True)
                    ins.then_inc(scores_done, 1)
                beside_unit(BESIDE2[u])
                if 2 <= u < UNITS + 2:
                    if u == 2:
                        pe.wait_ge(v_ready, 5)
                    turn_probs(g - 2, p2)
                if u >= LAG:
                    values(g - LAG, *unit2(u - LAG), pt2,
                           lambda h, j: v2[:, j, h // 4 * HD:(h // 4 + 1) * HD], lambda b: (b - 1, b))

            pe.wait_ge(heads_ready, 8)
            pe.wait_ge(conv_ready, 4)

            def branches(n):
                for m in range(2):
                    open_block(n, m)
                    for k in range(4):
                        step(MIX2 % 2, [m], k, lambda m, k: G(m, 4 * m + k), k == 0, k == 3)

            with pe.Fori(0, KC) as i:
                branches(MIX2 + 2 * i)
                panel(MIX2 + 2 * i + 1, MIX2 + 1, H)

            panel(OUT2, OUT2, G, merged_ready)
            panel(OUT2 + 1, OUT2 + 1, G)
            panels(OUT2, 2, G, first=1)
            ffn(FFN2, 3, FC)

            def turn_y(t):
                for k in range(KC):
                    ins = pe.transpose(ps[:, 2 * (t % 3) + k // 4, (k % 4) * P:(k % 4 + 1) * P],
                                       yT[:, k * T + t * P:k * T + (t + 1) * P], ident[:, :])
                ins.then_inc(y_turned, 1)

            pe.wait_ge(y_scaled, KC)
            pe.wait_ge(evacuated, 2 * PANELS)
            turn_y(0)
            pe.wait_ge(sq_added, 5 * KC)
            for t in range(NT):
                ins = pe.matmul(ps[:, 6, t:t + 1], sq_sum[:, t * P:(t + 1) * P], ones[:, 0:1], start=True, stop=True)
            ins.then_inc(norm_summed, 1)
            turn_y(1)
            turn_y(2)
            pe.wait_ge(y_vec, 1)
            pe.wait_ge(y_act, 1)
            turn_y(3)


_INS = ["x", "norm1_g", "w_in", "q_norm_g", "k_norm_g", "rpb", "w_pool", "pool_scale", "w_out", "norm2_g",
        "w_gate", "w_up", "w_down", "mix_norm_2", "w_in_2", "b_in_2", "sinks_2", "conv_w_2",
        "w_attn_branch_2", "w_conv_branch_2", "w_out_2", "ffn_norm_2", "w_up_2", "ffn_conv_w_2",
        "w_down_2", "final_norm_2"]


def kernel(**inputs):
    import numpy as np
    import concourse.bacc as bacc
    from concourse.bass_utils import run_bass_kernel_spmd

    nc = bacc.Bacc("TRN2", target_bir_lowering=False, num_devices=1)
    arrays, args = {}, []
    for name in _INS:
        a = np.ascontiguousarray(inputs[name])
        arrays["in_" + name] = a
        args.append(nc.dram_tensor("in_" + name, a.shape, mybir.dt.from_np(a.dtype), kind="ExternalInput").ap())
    shape = inputs["x"].shape
    args.append(nc.dram_tensor("out_0", shape, F32, kind="ExternalOutput").ap())
    two_blocks(nc, *args)
    r = run_bass_kernel_spmd(nc, [arrays], core_ids=[0])
    return r.results[0]["out_0"]
```

```python
from contextlib import ExitStack

import concourse.bass as bass
from concourse import mybir

ALU = mybir.AluOpType
ACT = mybir.ActivationFunctionType
F32 = mybir.dt.float32
F32R = mybir.dt.float32r
AX_X = mybir.AxisListType.X

P = 128
MASKED = -1e30


def two_blocks(
    nc, x, norm1_g, w_in, q_norm_g, k_norm_g, rpb, w_pool, pool_scale, w_out, norm2_g, w_gate, w_up,
    w_down, mix_norm_2, w_in_2, b_in_2, sinks_2, conv_w_2, w_attn_branch_2, w_conv_branch_2,
    w_out_2, ffn_norm_2, w_up_2, ffn_conv_w_2, w_down_2, final_norm_2, out,
):
    T, D = x.shape[1], x.shape[2]
    KC = D // P
    NT = T // P
    F = w_gate.shape[2]
    FC = F // P
    assert (T, D, F, w_up_2.shape[2]) == (512, 1024, 2816, 2 * F)
    HALF = KC * P
    GROUPS = [(g, min(KC, FC - g)) for g in range(0, FC, KC)]
    HEADS, HD = 8, 64
    GRID = 64
    ROWS = T // GRID
    RB, CB = rpb.shape[2], rpb.shape[3]
    UNITS = 16

    IN1 = 0
    OUT1 = IN1 + 2 * D // 256
    FFN1 = OUT1 + D // 256
    FFN_PANELS = FC + len(GROUPS) * D // 256
    IN2 = FFN1 + FFN_PANELS
    MIX2 = IN2 + 9
    OUT2 = MIX2 + 2 * KC
    FFN2 = OUT2 + D // 256
    PANELS = FFN2 + FFN_PANELS

    with ExitStack() as ctx:
        def sb(name, shape, dt=F32):
            return ctx.enter_context(nc.sbuf_tensor(name, shape, dt))

        def sem(name):
            return ctx.enter_context(nc.semaphore(name))

        ps = ctx.enter_context(nc.psum_tensor("ps", [P, 8, 512], F32))
        xT = sb("xT", [P, KC * T])
        h_hi = sb("h_hi", [P, KC * T], F32R)
        h_lo = sb("h_lo", [P, KC * T], F32R)
        g_hi = sb("g_hi", [P, KC * T], F32R)
        g_lo = sb("g_lo", [P, KC * T], F32R)
        w_stage = sb("w_stage", [P, 2, 2 * HALF])
        w_hi = sb("w_hi", [P, 2, 2 * HALF], F32R)
        w_lo = sb("w_lo", [P, 2, 2 * HALF], F32R)
        rs = sb("rs", [P, T])
        rms = sb("rms", [P, T])
        sq_sum = sb("sq_sum", [P, T])
        sq = sb("sq", [P, 2, T])
        ident = sb("ident", [P, P])
        ones = sb("ones", [P, P])
        head_ones = sb("head_ones", [P, P])
        eps = sb("eps", [P, 3])
        w_pool_sb = sb("w_pool_sb", [P, 4, P])
        inv_edge = sb("inv_edge", [P, 4, 2, 8])
        mask2 = sb("mask2", [P, 2, 2 * P])
        sink = sb("sink", [P, HEADS])
        neg_sink = sb("neg_sink", [P, HEADS])
        neg_max = sb("neg_max", [P, 2, 2])
        exp_sum = sb("exp_sum", [P, 2, 2])
        exp_sink = sb("exp_sink", [P, 2, 2])
        exp_all = sb("exp_all", [P, 2, 2])
        inv_sum = sb("inv_sum", [P, 2, 2])
        edge = sb("edge", [P, 2, 2, 8])
        rms_col = sb("rms_col", [P, NT])
        rs_col = sb("rs_col", [P, NT])
        vec_rows = sb("vec_rows", [P, 3, P])
        mid = sb("mid", [P, 14400])

        vec_of = {}
        vec_loads = []
        V_ROWS = [0, 0, 0]

        def vector_rows(name, tile, src):
            vec_of[name] = sum(V_ROWS[:tile]) + V_ROWS[tile]
            vec_loads.append((tile, V_ROWS[tile], src))
            V_ROWS[tile] += src.shape[0]

        for name, a in (("norm1", norm1_g[0]), ("norm2", norm2_g[0]), ("mix", mix_norm_2[0]),
                        ("ffn", ffn_norm_2[0]), ("final", final_norm_2), ("b_in", b_in_2[0]),
                        ("pool", pool_scale[0])):
            vector_rows(name, 0, a.rearrange("(r c) -> r c", c=P))
        vector_rows("conv", 0, conv_w_2[0].rearrange("t (r c) -> (t r) c", c=P))
        vec_of["q"] = V_ROWS[0]
        vec_of["k"] = V_ROWS[0] + 1
        Q_ROW = V_ROWS[0]
        V_ROWS[0] += 2
        taps = ffn_conv_w_2[0].rearrange("t (r c) -> t r c", c=P)
        FR = 2 * FC
        vector_rows("fconv0", 1, taps[0])
        vector_rows("fconv1", 1, taps[1])
        vector_rows("fconv2", 2, taps[2])
        NV = sum(V_ROWS)
        vec = sb("vec", [P, NV])

        def col(name, i=0):
            return vec[:, bass.ds(vec_of[name] + i, 1)]

        x_in = mid[:, 0:NT * D].rearrange("p (t d) -> p t d", t=NT)
        q1 = mid[:, 0:2048].rearrange("p (a t) -> p a t", a=4)
        k1 = mid[:, 2048:4096].rearrange("p (a t) -> p a t", a=4)
        v1 = mid[:, 4096:6144].rearrange("p (j c) -> p j c", j=4)
        bias = mid[:, 6144:10240]
        p1 = mid[:, 10240:11264].rearrange("p (b s) -> p b s", b=2)
        pt1 = mid[:, 11264:12288].rearrange("p (b s) -> p b s", b=2)
        PAD = 8
        U = T + 2 * PAD
        u_pad = mid[:, 12288:12288 + 2 * U].rearrange("p (b s) -> p b s", b=2)
        win = mid[:, 12288 + 2 * U:12288 + 4 * U].rearrange("p (b s) -> p b s", b=2)
        v_t = u_pad
        sq_start = mid[:, 6144:10240]
        BR = 256
        bias_in = mid[:, 4096:4096 + HEADS * BR].rearrange("p (h s) -> p h s", h=HEADS)
        bias_in_edge = mid[:, 12288:12288 + HEADS * BR].rearrange("p (h s) -> p h s", h=HEADS)
        q2 = mid[:, 0:2048].rearrange("p (a t) -> p a t", a=4)
        k2 = mid[:, 2048:3072].rearrange("p (a t) -> p a t", a=2)
        v2 = mid[:, 3072:3584].rearrange("p (n c) -> p n c", n=4)
        v2_t = mid[:, 3584:4096]
        p2 = mid[:, 4096:5120].rearrange("p (b s) -> p b s", b=2)
        pt2 = mid[:, 5120:6144].rearrange("p (b s) -> p b s", b=2)
        cb = mid[:, 6144:8192].rearrange("p (a t) -> p a t", a=4)
        cc = mid[:, 8192:10240].rearrange("p (a t) -> p a t", a=4)
        CZ = T + 4
        cz = mid[:, 10240:10240 + 2 * CZ].rearrange("p (b s) -> p b s", b=2)
        cy = mid[:, 11272:12296].rearrange("p (b s) -> p b s", b=2)
        cx = mid[:, 12296:13320].rearrange("p (b s) -> p b s", b=2)
        merged = mid[:, 0:4096]
        branch = mid[:, 4096:5120].rearrange("p (b s) -> p b s", b=2)
        gates = mid[:, 5120:6144].rearrange("p (b s) -> p b s", b=2)
        yT = mid[:, 0:4096]
        y_out = mid[:, 4096:8192].rearrange("p (t d) -> p t d", t=NT)
        f_in = mid[:, 8400:8400 + 4 * CZ].rearrange("p (b s) -> p b s", b=4)
        f_cv = mid[:, 10464:10464 + 4 * T].rearrange("p (b s) -> p b s", b=4)

        x_landed = [sem(f"x_landed{t}") for t in range(NT)]
        norm1_landed = sem("norm1_landed")
        norm1_turned = sem("norm1_turned")
        norm1_ready = sem("norm1_ready")
        vec_landed = sem("vec_landed")
        bias_landed = sem("bias_landed")
        pool_w_landed = sem("pool_w_landed")
        w_landed = [[sem(f"w_landed{s}{m}") for m in range(2)] for s in range(2)]
        w_hi_ready = sem("w_hi_ready")
        w_lo_ready = sem("w_lo_ready")
        mm_done = sem("mm_done")
        evacuated = sem("evacuated")
        const_step = sem("const_step")
        bias_cleared = sem("bias_cleared")
        bias_step = sem("bias_step")
        bias_ready = sem("bias_ready")
        edge_ready = sem("edge_ready")
        mask_ready = sem("mask_ready")
        vec_turned = sem("vec_turned")
        vec_ready = sem("vec_ready")
        x_turned = sem("x_turned")
        x_ready = sem("x_ready")
        x_scaled = sem("x_scaled")
        x_squared = sem("x_squared")
        sum_cleared = sem("sum_cleared")
        sq_added = sem("sq_added")
        h_ready = sem("h_ready")
        norm_summed = sem("norm_summed")
        norm_rooted = sem("norm_rooted")
        rs_ready = sem("rs_ready")
        qk_squared = sem("qk_squared")
        qk_summed = sem("qk_summed")
        qk_rooted = sem("qk_rooted")
        qk_inverted = sem("qk_inverted")
        qk_ready = sem("qk_ready")
        v_turned = sem("v_turned")
        v_ready = sem("v_ready")
        scores_done = sem("scores_done")
        scores_read = sem("scores_read")
        exp_done = sem("exp_done")
        sink_done = sem("sink_done")
        sum_ready = sem("sum_ready")
        inv_ready = sem("inv_ready")
        probs_ready = sem("probs_ready")
        probs_turned = sem("probs_turned")
        pt_ready = sem("pt_ready")
        pv_done = sem("pv_done")
        heads_hi = sem("heads_hi")
        heads_ready = sem("heads_ready")
        pads_cleared = sem("pads_cleared")
        win_step = sem("win_step")
        pool_in = sem("pool_in")
        pool_mm = sem("pool_mm")
        pool_hi = sem("pool_hi")
        pool_ready = sem("pool_ready")
        in2_biased = sem("in2_biased")
        k2_ready = sem("k2_ready")
        cz_ready = sem("cz_ready")
        tap_act = sem("tap_act")
        tap_vec = sem("tap_vec")
        conv_gated = sem("conv_gated")
        conv_hi = sem("conv_hi")
        conv_ready = sem("conv_ready")
        gate_done = sem("gate_done")
        mix_step = sem("mix_step")
        merged_hi = sem("merged_hi")
        merged_ready = sem("merged_ready")
        f_tap_act = sem("f_tap_act")
        f_tap_vec = sem("f_tap_vec")
        f_silu = sem("f_silu")
        f_prod = sem("f_prod")
        f_hi = sem("f_hi")
        f_ready = sem("f_ready")
        y_scaled = sem("y_scaled")
        waits_passed = sem("waits_passed")
        y_turned = sem("y_turned")
        y_vec = sem("y_vec")
        y_act = sem("y_act")
        out_landed = sem("out_landed")

        def chunk(t, k):
            return t[:, bass.ds(k * T, T)]

        def low_of(t):
            return t.bitcast(F32)

        def bank(n, m):
            return ps[:, (2 * (n % 2) if n >= 0 else 6) + m, :]

        def static(n):
            return isinstance(n, int)

        def ffn_plan(base):
            plan, n = [], base
            for f0, nf in GROUPS:
                plan.append((n, n + nf, f0, nf))
                n += nf + D // 256
            return plan

        LAG = 3
        SPAN = UNITS + LAG

        def beside(first, count, units):
            steps = [(n, m, k) for n in range(first, first + count) for m in range(2)
                     for k in range(0, KC, 2)]
            cut = [len(steps) * u // units for u in range(units + 1)]
            return [steps[a:b] for a, b in zip(cut, cut[1:])] + [[] for _ in range(SPAN - units)]

        steps1 = [s for steps in beside(IN1 + 6, 2, 1) for s in steps]
        BESIDE1 = [steps1[:4]] + [steps1[4 + 12 * u // 10:4 + 12 * (u + 1) // 10] for u in range(10)]
        BESIDE1 += [[] for _ in range(SPAN - len(BESIDE1))]
        AFTER = 2
        BESIDE2 = beside(IN2 + 4, 5, SPAN) + [[] for _ in range(AFTER)]
        IN2_ORDER = (0, 1, 2, 3, 5, 7, 6, 8, 4)
        CONV_PART = {IN2 + 3: (0, 0), IN2 + 4: (1, 0), IN2 + 5: (2, 0),
                     IN2 + 6: (1, 1), IN2 + 7: (2, 1), IN2 + 8: (0, 1)}

        def ends(part):
            return [u for u, steps in enumerate(BESIDE2) for n, m, k in steps
                    if CONV_PART[n][0] == part and k == KC - 2]

        CX_END, CB_END = ends(2), [0, 0] + ends(0)
        CONV_AT = [(x + 1, x + 2, max(x + 3, y + 1), max(x + 3, y + 1) + 1) for x, y in zip(CX_END, CB_END)]
        SUMS_AT, MEANS_AT, POOL_AT = {0: 0, 4: 1, 7: 2, 11: 3}, {2: 0, 5: 1, 8: 2, 12: 3}, {3: 0, 6: 1, 10: 2, 15: 3}

        def probs(p, u):
            return p[:, u % 4, :] if u % 4 < 2 else sq[:, u % 4 - 2, :]

        def unit1(u):
            return u // 2, ((3, 0) if u % 2 == 0 else (1, 2))

        def keys1(b):
            return (b - 1, b) if b else (0, 3)

        def unit2(u):
            return u // 2, ((0, 1) if u % 2 == 0 else (2, 3))

        def inner(ap):
            return ap.rearrange("p (w x) -> p w x", x=GRID)[:, :, 8:56].rearrange("p w (b c) -> p b w c", c=16)

        def border(ap):
            return ap.rearrange("p (w e c) -> p w e c", e=8, c=8)[:, :, 0:8:7, :]

        def rows_up(ap, dim):
            dims = [list(d) for d in ap.ap]
            offset = ap.offset + (ROWS - 1) * dims[dim][0]
            dims[dim][0] = -dims[dim][0]
            return bass.AP(ap.tensor, offset, dims)

        def inner_q(ap):
            return rows_up(ap[:, P:T].rearrange("p (b c w) -> p b w c", b=3, c=16), 2)

        def border_q(ap):
            return rows_up(ap[:, 0:P].rearrange("p (e c w) -> p w e c", e=2, c=8), 1)

        def by_chunk(ap):
            return ap.rearrange("p (w j c) -> p j w c", j=4, c=16)

        def twice(ap):
            return bass.AP(ap.tensor, ap.offset, [list(ap.ap[0]), [0, 2], list(ap.ap[-1])])

        block = ctx.enter_context(nc.Block())

        @block.sync
        def _(sp):
            for t in range(NT):
                sp.dma_start(x_in[:, t, :], x[0, t * P:(t + 1) * P, :]).then_inc(x_landed[t], 16)

            def load(n, s, srcs, chunks=KC):
                for m, src in enumerate(srcs):
                    if not static(n) or n >= 2:
                        sp.wait_ge(w_lo_ready, 2 * n + m - 3)
                    sp.dma_start(
                        w_stage[:, s, m * HALF:(m + 1) * HALF].rearrange("p (k c) -> p k c", c=P)[:, 0:chunks, :],
                        src.rearrange("(k p) c -> p k c", p=P)).then_inc(w_landed[s][m], 16)

            def cols(w, c):
                return w[:, bass.ds(c, P)]

            def load_pairs(n0, panels, w, c0):
                with sp.Fori(0, panels // 2) as i:
                    for j in range(2):
                        c = c0 + i * 512 + j * 256
                        load(n0 + 2 * i + j, (n0 + j) % 2, [cols(w, c), cols(w, c + P)],
                             w.shape[0] // P)

            def load_ffn(base, w_g, w_u, up0, w_d):
                for n0, nd, f0, nf in ffn_plan(base):
                    with sp.Fori(0, nf // 2) as i:
                        for j in range(2):
                            c = i * 256 + (f0 + j) * P
                            load(n0 + 2 * i + j, (n0 + j) % 2, [cols(w_g, c), cols(w_u, c + up0)])
                    load_pairs(nd, D // 256, w_d[f0 * P:(f0 + nf) * P, :], 0)

            for n in range(2):
                load(IN1 + n, n % 2, [cols(w_in[0], n * 256), cols(w_in[0], n * 256 + P)])
            for tile, r, src in vec_loads[1:]:
                sp.dma_start(vec_rows[r:r + src.shape[0], tile, :], src).then_inc(vec_landed, 16)
            for i, g in enumerate((q_norm_g, k_norm_g)):
                for e in range(2):
                    sp.dma_start(vec_rows[Q_ROW + i:Q_ROW + i + 1, 0, e * HD:(e + 1) * HD], g)\
                      .then_inc(vec_landed, 16)
            sp.dma_start(sink[:, :], bass.AP(sinks_2.tensor, sinks_2.offset, [[0, P], [1, HEADS]]))\
              .then_inc(vec_landed, 16)
            for n in range(2, 4):
                load(IN1 + n, n % 2, [cols(w_in[0], n * 256), cols(w_in[0], n * 256 + P)])
            sp.wait_ge(bias_cleared, 1)
            run = (ROWS - 1) * CB + 16
            for c in range(16):
                for dst, shift, first in ((bias_in, c, 7), (bias_in_edge, 0, 15 - c)):
                    sp.dma_start(dst[c * ROWS:(c + 1) * ROWS, :, shift:shift + run],
                                 bass.AP(rpb.tensor, rpb.offset + first,
                                         [[CB, ROWS], [RB * CB, HEADS], [1, run]])).then_inc(bias_landed, 16)
            sp.dma_start(w_pool_sb[:, :, :], w_pool[0].rearrange("g c d -> c g d")).then_inc(pool_w_landed, 16)
            load_pairs(IN1 + 4, 4, w_in[0], 1024)
            load_pairs(OUT1, D // 256, w_out[0], 0)
            load_ffn(FFN1, w_gate[0], w_up[0], 0, w_down[0])
            for i, p in enumerate(IN2_ORDER):
                load(IN2 + i, (IN2 + i) % 2, [cols(w_in_2[0], 256 * p), cols(w_in_2[0], 256 * p + P)])
            with sp.Fori(0, KC) as i:
                c = i * P
                load(MIX2 + 2 * i, MIX2 % 2,
                     [cols(w_attn_branch_2[0], c), cols(w_conv_branch_2[0], c)], 4)
                load(MIX2 + 2 * i + 1, (MIX2 + 1) % 2,
                     [cols(w_in_2[0], c + 2304), cols(w_in_2[0], c + 2304 + D)])
            load_pairs(OUT2, D // 256, w_out_2[0], 0)
            load_ffn(FFN2, w_up_2[0], w_up_2[0], F, w_down_2[0])
            for t in range(NT):
                sp.wait_ge(y_vec, t + 1)
                sp.wait_ge(y_act, t + 1)
                sp.dma_start(out[0, t * P:(t + 1) * P, :], y_out[:, t, :]).then_inc(out_landed, 16)
            sp.wait_ge(out_landed, 16 * NT)

        @block.gpsimd
        def _(pool):
            def select(ap, in_, base, pattern, mult, cmp=ALU.is_ge, fill=MASKED):
                return pool.affine_select(out=ap, in_=in_, compare_op=cmp, fill=fill, base=base,
                                          pattern=pattern, channel_multiplier=mult)

            def low_part(n, s):
                for m in range(2):
                    pool.wait_ge(w_hi_ready, 2 * n + m + 1)
                    c = slice(m * HALF, (m + 1) * HALF)
                    pool.tensor_tensor(w_lo[:, s, c], w_stage[:, s, c], low_of(w_hi[:, s, c]),
                                       ALU.subtract).then_inc(w_lo_ready, 1)

            pool.memset(ident[:, :], 0.0).then_inc(const_step, 1)
            pool.wait_ge(const_step, 1)
            select(ident[:, :], ident[:, :], 0, [[-1, P]], 1, ALU.not_equal, 1.0).then_inc(const_step, 1)
            pool.memset(eps[:, 0:1], 1e-6)
            pool.memset(eps[:, 1:2], 1e-5)
            pool.memset(eps[:, 2:3], HD * 1e-6)
            pool.memset(ones[:, :], 1.0)
            pool.memset(head_ones[:, :], 0.0).then_inc(const_step, 1)
            pool.wait_ge(const_step, 3)
            pool.memset(head_ones[0:HD, 0:HD], 1.0)
            pool.memset(head_ones[HD:P, HD:P], 1.0).then_inc(const_step, 1)
            pool.wait_ge(const_step, 4)
            pool.memset(bias_in[:, :, :], 0.0)
            pool.memset(bias_in_edge[:, :, :], 0.0).then_inc(bias_cleared, 1)
            for n in range(5):
                low_part(n, n % 2)

            pool.wait_ge(bias_landed, 16 * 2 * 16)
            pool.wait_ge(sq_added, KC)
            for h in range(HEADS):
                rows = bias_in[:, h, 0:ROWS * CB].rearrange("p (w k) -> p w k", k=CB)
                edges = bias_in_edge[:, h, 0:ROWS * CB].rearrange("p (w k) -> p w k", k=CB)[:, :, 0:16]
                o = [bias[:, (4 * h + s) * P:(4 * h + s + 1) * P].rearrange("p (w k) -> p w k", k=16)
                     for s in range(4)]
                select(o[0], rows[:, :, 0:16], ROWS - 1, [[0, ROWS], [ROWS, 16]], -1)
                select(o[1][:, :, 0:15], rows[:, :, 16:31], -ROWS, [[0, ROWS], [-ROWS, 15]], 1)
                pool.memset(o[1][:, :, 15:16], MASKED)
                select(o[2], edges, P // 2 - 1, [[0, ROWS], [0, 16]], -1)
                last = select(o[3], edges, -P // 2, [[0, ROWS], [0, 16]], 1)
            last.then_inc(bias_ready, 1)
            low_part(5, 1)

            for g in range(4):
                w = 1 << g
                pool.memset(inv_edge[:, g, 0, w:8], 0.5 / w) if w < 8 else None
                pool.memset(inv_edge[:, g, 1, 0:9 - w], 0.5 / w)
                for i in range(w):
                    pool.memset(inv_edge[:, g, 0, i:i + 1], 1.0 / (w + i))
                for i in range(9 - w, 8):
                    pool.memset(inv_edge[:, g, 1, i:i + 1], 1.0 / (w + 8 - i))
            pool.memset(mask2[:, 0, 0:P], MASKED)
            pool.memset(mask2[:, 0, P:2 * P], 0.0)
            pool.memset(mask2[:, 1, :], 0.0).then_inc(edge_ready, 1)
            pool.wait_ge(edge_ready, 1)
            select(mask2[:, 1, 0:P], mask2[:, 1, 0:P], -1, [[1, P]], -1)
            select(mask2[:, 1, P:2 * P], mask2[:, 1, P:2 * P], 0, [[-1, P]], 1)
            select(mask2[:, 0, P:2 * P], mask2[:, 0, P:2 * P], 0, [[-1, P]], 1).then_inc(mask_ready, 1)

            with pool.Fori(3, PANELS // 2) as i:
                for j in range(2):
                    low_part(2 * i + j, j)
            low_part(PANELS - 1, (PANELS - 1) % 2)

        @block.scalar
        def _(act):
            tile, r, src = vec_loads[0]
            act.dma_start(vec_rows[r:r + src.shape[0], tile, :], src).then_inc(norm1_landed, 16)

            def wait_apart(signal, value):
                act.wait_ge(signal, value)
                act.sem_inc(waits_passed, 1)

            def high_part(n, s, m):
                act.wait_ge(w_landed[s][m], 8 * n - 8 * s + 16)
                if not static(n) or n >= 2:
                    act.wait_ge(mm_done, 2 * n + m - 3)
                c = slice(m * HALF, (m + 1) * HALF)
                act.activation(w_hi[:, s, c], w_stage[:, s, c], ACT.Copy).then_inc(w_hi_ready, 1)

            def ahead(n, s, blocks=(0, 1)):
                if not static(n) or n + 2 < PANELS:
                    for m in blocks:
                        high_part(n + 2, s, m)

            def norm_chunk(r, m, par, gain):
                act.activation(chunk(h_hi, m), chunk(xT, m), ACT.Copy, scale=col(gain, m)).then_inc(x_scaled, 1)
                if r or m >= 2:
                    wait_apart(sq_added, KC * r + m - 1)
                act.activation(sq[:, par, :], chunk(xT, m), ACT.Square).then_inc(x_squared, 1)

            def norm_root(r):
                act.wait_ge(norm_summed, r + 1)
                e = 0 if r < 2 else 1
                act.activation(rms[:, :], ps[:, 4, :], ACT.Sqrt, scale=1.0 / D,
                               bias=eps[:, e:e + 1]).then_inc(norm_rooted, 1)

            act.wait_ge(const_step, 3)
            act.wait_ge(norm1_ready, 1)
            for m in range(KC):
                act.wait_ge(x_ready, m + 1)
                act.activation(chunk(h_hi, m), chunk(xT, m), ACT.Copy, scale=col("norm1", m)).then_inc(x_scaled, 1)
                if m < 2:
                    high_part(0, 0, m)
            high_part(1, 1, 0)
            high_part(1, 1, 1)
            for m in range(KC):
                act.activation(chunk(sq_start, m), chunk(xT, m), ACT.Square).then_inc(x_squared, 1)

            def qk_squares(n):
                for c in (2 * n, 2 * n + 1):
                    act.wait_ge(evacuated, c + 1)
                    if c >= 2:
                        act.wait_ge(qk_summed, c - 1)
                    act.activation(p1[:, c % 2, :], (q1 if c < 4 else k1)[:, c % 4, :],
                                   ACT.Square).then_inc(qk_squared, 1)

            def qk_roots(n):
                for c in (2 * n, 2 * n + 1):
                    act.wait_ge(qk_summed, c + 1)
                    if c >= 2:
                        act.wait_ge(qk_ready, c - 1)
                    act.activation(pt1[:, c % 2, :], ps[:, 5 + c % 2, :], ACT.Sqrt,
                                   scale=1.0 if c < 4 else 1.0 / HD,
                                   bias=eps[:, 2:3] if c < 4 else eps[:, 0:1]).then_inc(qk_rooted, 1)

            norm_root(0)
            ahead(0, 0)
            qk_squares(0)
            for n in range(1, 4):
                ahead(n, n % 2)
                qk_squares(n)
                qk_roots(n - 1)
            ahead(4, 0)
            qk_roots(3)
            ahead(5, 1)

            def exps(u, p):
                act.wait_ge(scores_read, u + 1)
                for i in range(2):
                    q = probs(p, u)[:, i * 256:(i + 1) * 256]
                    act.activation(q, q, ACT.Exp, scale=-1.0, bias=neg_max[:, u % 2, i:i + 1],
                                   accum_out=exp_sum[:, u % 2, i:i + 1]).then_inc(exp_done, 1)

            def copy_pt(u, pt):
                act.wait_ge(probs_turned, u + 1)
                if u >= 2:
                    act.wait_ge(pv_done, u - 1)
                act.activation(pt[:, u % 2, :], ps[:, 6, :], ACT.Copy).then_inc(pt_ready, 1)

            for u in range(SPAN):
                if u < UNITS:
                    exps(u, p1)
                if 2 <= u < UNITS + 2:
                    copy_pt(u - 2, pt1)
                if u >= 6 and u % 4 == 2:
                    a = (u - 6) // 4
                    act.wait_ge(pv_done, 4 * a + 4)
                    act.activation(inner(chunk(g_hi, a)), inner_q(ps[:, 7, :]), ACT.Copy)
                    act.activation(border(chunk(g_hi, a)), border_q(ps[:, 7, :]), ACT.Copy).then_inc(heads_hi, 1)
                for n, m, k in BESIDE1[u]:
                    if k == KC - 2:
                        ahead(n, n % 2, [m])
                if u in POOL_AT:
                    g = POOL_AT[u]
                    act.wait_ge(pool_mm, g + 1)
                    act.activation(chunk(g_hi, 4 + g), ps[:, g, :], ACT.Copy, scale=col("pool", g))\
                       .then_inc(pool_hi, 1)

            def update_norm(n0, r, gain):
                with act.Fori(0, 2) as i:
                    for j in range(2):
                        n = n0 + 2 * i + j
                        for e in range(2):
                            m = 4 * i + 2 * j + e
                            if gain != "final":
                                ahead(n, (n0 + j) % 2, [e])
                            wait_apart(evacuated, 2 * n + e + 1)
                            if gain == "final":
                                act.activation(chunk(yT, m), chunk(xT, m), ACT.Copy, scale=col(gain, m))\
                                   .then_inc(y_scaled, 1)
                                wait_apart(sq_added, KC * r + m - 1)
                                act.activation(sq[:, e, :], chunk(xT, m), ACT.Square).then_inc(x_squared, 1)
                            else:
                                norm_chunk(r, m, e, gain)

            def ffn(base, r, second):
                done = FC if second else 0
                for gi, (n0, nd, f0, nf) in enumerate(ffn_plan(base)):
                    if gi == 0:
                        norm_root(r)
                    with act.Fori(0, nf // 2) as i:
                        for j in range(2):
                            n = n0 + 2 * i + j
                            f = done + f0 + j + 2 * i
                            gate, up = (f_cv if second else f_in)[:, j, 0:T], (f_cv if second else f_in)[:, 2 + j, 0:T]
                            ahead(n, (n0 + j) % 2)
                            wait_apart(evacuated, 2 * n + 1)
                            if second:
                                c = f0 + j + 2 * i
                                act.activation(gate, f_in[:, j, 2:2 + T], ACT.Copy,
                                               scale=col("fconv2", c)).then_inc(f_tap_act, 1)
                                wait_apart(evacuated, 2 * n + 2)
                                act.activation(up, f_in[:, 2 + j, 2:2 + T], ACT.Copy,
                                               scale=col("fconv2", c + FC)).then_inc(f_tap_act, 1)
                                act.wait_ge(f_tap_vec, 4 * (f - FC) + 3)
                            act.activation(gate, gate, ACT.Silu).then_inc(f_silu, 1)
                            wait_apart(f_prod, f + 1)
                            act.activation(chunk(g_hi, 2 * i + j), up, ACT.Copy).then_inc(f_hi, 1)
                    if gi < len(GROUPS) - 1:
                        with act.Fori(0, 2) as i:
                            for j in range(2):
                                ahead(nd + 2 * i + j, (nd + j) % 2)
                    elif not second:
                        update_norm(nd, 2, "mix")
                    else:
                        ahead(nd, nd % 2)
                        ahead(nd + 1, (nd + 1) % 2)
                        update_norm(nd, 4, "final")

            update_norm(OUT1, 1, "norm2")
            ffn(FFN1, 1, False)

            def add_bias(ap, n, m, b):
                act.wait_ge(evacuated, 2 * n + m + 1)
                act.activation(ap, ap, ACT.Identity, bias=col("b_in", b)).then_inc(in2_biased, 1)

            norm_root(2)
            for n in range(3):
                ahead(IN2 + n, (IN2 + n) % 2)
                for m in range(2):
                    j = 2 * n + m
                    add_bias(q2[:, j, :] if j < 4 else (k2[:, 0, :] if j == 4 else v2_t), IN2 + n, m, j)
            ahead(IN2 + 3, (IN2 + 3) % 2)

            for u in range(SPAN + AFTER):
                g = UNITS + u
                if u < UNITS:
                    exps(g, p2)
                    act.activation(exp_sink[:, g % 2, :], neg_max[:, g % 2, :], ACT.Exp,
                                   bias=sink[:, u // 2:u // 2 + 1]).then_inc(sink_done, 1)
                if 2 <= u < UNITS + 2:
                    copy_pt(g - 2, pt2)
                if u >= 6 and u % 4 == 2:
                    a = (u - 6) // 4
                    act.wait_ge(pv_done, UNITS + 4 * a + 4)
                    act.activation(chunk(g_hi, a), ps[:, 7, :], ACT.Copy).then_inc(heads_hi, 1)
                for c, at in enumerate(CONV_AT):
                    if u == at[0]:
                        act.wait_ge(cz_ready, c + 1)
                        act.activation(cy[:, c % 2, :], cz[:, c % 2, 2:2 + T], ACT.Copy,
                                       scale=col("conv", 8 + c)).then_inc(tap_act, 1)
                    elif u == at[2]:
                        act.wait_ge(conv_gated, c + 1)
                        act.activation(chunk(g_hi, 4 + c), cy[:, c % 2, :], ACT.Copy).then_inc(conv_hi, 1)
                for n, m, k in BESIDE2[u]:
                    if k == KC - 2:
                        ahead(n, n % 2, [m])
                        part, half = CONV_PART[n]
                        if part == 2:
                            add_bias(cx[:, m, :], n, m, 14 + 2 * half + m)

            def gate_pair(m):
                for e in range(2):
                    wait_apart(evacuated, 2 * MIX2 + 4 * m + 3 + e)
                    act.activation(gates[:, e, :], gates[:, e, :], ACT.Sigmoid,
                                   bias=col("b_in", 18 + KC * e + m)).then_inc(gate_done, 1)

            def merged_high(m):
                act.wait_ge(mix_step, 3 * m + 3)
                act.activation(chunk(g_hi, m), chunk(merged, m), ACT.Copy).then_inc(merged_hi, 1)

            with act.Fori(0, KC - 1) as i:
                ahead(MIX2 + 2 * i, MIX2 % 2)
                gate_pair(i)
                ahead(MIX2 + 1 + 2 * i, (MIX2 + 1) % 2)
            ahead(OUT2 - 2, OUT2 % 2)
            for m in range(KC - 1):
                merged_high(m)
            gate_pair(KC - 1)
            ahead(OUT2 - 1, (OUT2 - 1) % 2)
            merged_high(KC - 1)

            update_norm(OUT2, 3, "ffn")
            ffn(FFN2, 3, True)
            act.wait_ge(norm_summed, 5)
            act.activation(rms_col[:, :], ps[:, 6, 0:NT], ACT.Sqrt, scale=1.0 / D, bias=eps[:, 1:2])\
               .then_inc(norm_rooted, 1)
            act.wait_ge(rs_ready, 5)
            for t in range(NT):
                act.wait_ge(y_turned, t + 1)
                act.activation(y_out[:, t, 0:512], ps[:, 2 * (t % 3), :], ACT.Copy, scale=rs_col[:, t:t + 1])\
                   .then_inc(y_act, 1)

        @block.vector
        def _(dve):
            def take_in(n, m, par, out):
                dve.wait_ge(mm_done, 2 * n + m + 1)
                dve.tensor_tensor(out, bank(par, m), rs[:, :], ALU.mult).then_inc(evacuated, 1)

            def add_squares(r, m, squares):
                dve.wait_ge(x_squared, KC * r + m + 1)
                if not static(m) or m:
                    dve.wait_ge(sq_added, KC * r + m)
                dve.wait_ge(sum_cleared, r + 1)
                dve.tensor_tensor(sq_sum[:, :], sq_sum[:, :], squares, ALU.add).then_inc(sq_added, 1)

            def x_low(r, m, gain):
                dve.wait_ge(x_scaled, KC * r + m + 1)
                dve.scalar_tensor_tensor(chunk(h_lo, m), chunk(xT, m), col(gain, m),
                                         low_of(chunk(h_hi, m)), ALU.mult, ALU.subtract)\
                   .then_inc(h_ready, 1)

            def norm_low(r, m, par, gain):
                x_low(r, m, gain)
                add_squares(r, m, sq[:, par, :])

            def norm_factor(r):
                dve.wait_ge(norm_rooted, r + 1)
                dve.reciprocal(rs[:, :], rms[:, :]).then_inc(rs_ready, 1)
                dve.memset(sq_sum[:, :], 0.0).then_inc(sum_cleared, 1)
                dve.wait_ge(rs_ready, r + 1)

            dve.memset(sq_sum[:, :], 0.0).then_inc(sum_cleared, 1)
            dve.wait_ge(norm1_turned, 1)
            dve.tensor_copy(vec[:, 0:KC], ps[:, 5, 0:KC]).then_inc(norm1_ready, 1)
            for m in range(KC):
                dve.wait_ge(x_turned, m + 1)
                dve.tensor_copy(chunk(xT, m), ps[:, m % 4, :]).then_inc(x_ready, 1)
                if m:
                    x_low(0, m - 1, "norm1")
            x_low(0, KC - 1, "norm1")
            for m in range(KC):
                add_squares(0, m, chunk(sq_start, m))
            dve.wait_ge(vec_turned, 1)
            dve.tensor_copy(vec[:, KC:NV], ps[:, 5, KC:NV])
            dve.tensor_scalar(neg_sink[:, :], sink[:, :], -1.0, None, ALU.mult).then_inc(vec_ready, 1)
            norm_factor(0)
            dve.wait_ge(vec_ready, 1)

            def qk_take(n):
                for m in range(2):
                    c = 2 * n + m
                    if c >= 4:
                        take_in(n, m, n, k1[:, c - 4, :])
                        continue
                    dve.wait_ge(mm_done, c + 1)
                    b = bank(n or -1, m)
                    dve.tensor_tensor(inner_q(q1[:, c, :]), inner(b), inner(rs[:, :]), ALU.mult)
                    dve.tensor_tensor(border_q(q1[:, c, :]), border(b), border(rs[:, :]),
                                      ALU.mult).then_inc(evacuated, 1)

            def qk_norm(n):
                for c in (2 * n, 2 * n + 1):
                    dve.wait_ge(qk_rooted, c + 1)
                    dve.reciprocal(pt1[:, c % 2, :], pt1[:, c % 2, :]).then_inc(qk_inverted, 1)
                    dve.wait_ge(qk_inverted, c + 1)
                    x_ = (q1 if c < 4 else k1)[:, c % 4, :]
                    dve.scalar_tensor_tensor(x_, x_, col("q" if c < 4 else "k"), pt1[:, c % 2, :],
                                             ALU.mult, ALU.mult).then_inc(qk_ready, 1)

            def v_take(n):
                for m in range(2):
                    a = 2 * (n - 4) + m
                    if a >= 2:
                        dve.wait_ge(v_turned, a - 1)
                    dve.wait_ge(mm_done, 2 * n + m + 1)
                    dve.tensor_tensor(v_t[:, m, 0:T].rearrange("p (j w c) -> p j w c", j=4, c=16),
                                      by_chunk(bank(n, m)), by_chunk(rs[:, :]), ALU.mult).then_inc(evacuated, 1)

            def v_copy(a):
                dve.wait_ge(v_turned, a + 1)
                dve.tensor_copy(v1[:, :, a * P:(a + 1) * P],
                                ps[:, 6 + a % 2, :].rearrange("p (j c) -> p j c", j=4)).then_inc(v_ready, 1)

            def normalise(u, p):
                i = u % 2
                dve.wait_ge(exp_done, 2 * u + 2)
                total = exp_sum[:, i, :]
                if u >= UNITS:
                    dve.wait_ge(sink_done, u - UNITS + 1)
                    dve.tensor_tensor(exp_all[:, i, :], total, exp_sink[:, i, :], ALU.add).then_inc(sum_ready, 1)
                    dve.wait_ge(sum_ready, u - UNITS + 1)
                    total = exp_all[:, i, :]
                dve.reciprocal(inv_sum[:, i, :], total).then_inc(inv_ready, 1)
                dve.wait_ge(inv_ready, u + 1)
                for b in range(2):
                    q = probs(p, u)[:, b * 256:(b + 1) * 256]
                    ins = dve.tensor_scalar(q, q, inv_sum[:, i, b:b + 1], None, ALU.mult)
                ins.then_inc(probs_ready, 1)

            def negated_scores(u, p, tables, factor, bound):
                for i, table in enumerate(tables):
                    c = slice(i * 256, (i + 1) * 256)
                    ins = dve.tensor_tensor_reduce(
                        out=probs(p, u)[:, c], in0=ps[:, 4 + u % 2, c], in1=table, scale=-factor,
                        scalar=bound, op0=ALU.add, op1=ALU.min, accum_out=neg_max[:, u % 2, i:i + 1])
                ins.then_inc(scores_read, 1)

            qk_take(0)
            for n in range(1, 4):
                qk_take(n)
                qk_norm(n - 1)
            dve.wait_ge(bias_ready, 1)
            v_take(4)
            qk_norm(3)
            v_copy(0)
            v_copy(1)
            v_take(5)

            def pool_sums(n, m):
                g = 2 * (n - 6) + m
                if g >= 2:
                    dve.wait_ge(pool_mm, g - 1)
                body = u_pad[:, m, PAD:PAD + T]
                take_in(n, m, n, body)
                dve.wait_ge(evacuated, 2 * n + m + 1)
                src, n_in = u_pad[:, m, :], U
                for k in range(g + 1):
                    d = 1 << k
                    o = win[:, k % 2, 0:n_in - d]
                    dve.tensor_tensor(o, src[:, 0:n_in - d], src[:, d:n_in], ALU.add).then_inc(win_step, 1)
                    dve.wait_ge(win_step, steps_before(g) + k + 1)
                    src, n_in = win[:, k % 2, :], n_in - d

            def pool_means(g):
                m = g % 2
                body = u_pad[:, m, PAD:PAD + T]
                w = 1 << g
                sums = win[:, m, PAD - w:PAD - w + T]

                def ends(ap):
                    return ap.rearrange("p (b x) -> p b x", x=8)[:, 0:64:63, :]

                dve.tensor_tensor(edge[:, m, :, :], ends(sums), inv_edge[:, g, :, :], ALU.mult).then_inc(win_step, 1)
                dve.wait_ge(win_step, steps_before(g) + g + 2)
                dve.tensor_tensor(edge[:, m, :, :], edge[:, m, :, :], ends(body), ALU.subtract).then_inc(win_step, 1)
                dve.wait_ge(win_step, steps_before(g) + g + 3)
                dve.scalar_tensor_tensor(body, sums, 0.5 / w, body, ALU.mult, ALU.subtract).then_inc(win_step, 1)
                dve.wait_ge(win_step, steps_before(g) + g + 4)
                dve.tensor_copy(ends(body), edge[:, m, :, :]).then_inc(pool_in, 1)

            def steps_before(g):
                return sum(4 + i for i in range(g))

            for u in range(SPAN):
                if u < UNITS:
                    h, bs = unit1(u)
                    dve.wait_ge(scores_done, u + 1)
                    if u >= 4:
                        dve.wait_ge(probs_turned, u - 3)
                    at = [bias[:, (2 * h + s) * 256:(2 * h + s + 1) * 256] for s in range(2)]
                    negated_scores(u, p1, [at[b == 0] for b in bs], 1.0, -4 * MASKED)
                if u == 0:
                    v_copy(2)
                    v_copy(3)
                    dve.memset(u_pad[:, :, 0:PAD], 0.0)
                    dve.memset(u_pad[:, :, PAD + T:U], 0.0).then_inc(pads_cleared, 1)
                    dve.wait_ge(pads_cleared, 1)
                    dve.wait_ge(edge_ready, 1)
                if 1 <= u <= UNITS:
                    normalise(u - 1, p1)
                if u >= 6 and u % 4 == 2:
                    a = (u - 6) // 4
                    dve.wait_ge(heads_hi, a + 1)
                    dve.tensor_tensor(inner(chunk(g_lo, a)), inner_q(ps[:, 7, :]),
                                      inner(low_of(chunk(g_hi, a))), ALU.subtract)
                    dve.tensor_tensor(border(chunk(g_lo, a)), border_q(ps[:, 7, :]),
                                      border(low_of(chunk(g_hi, a))), ALU.subtract).then_inc(heads_ready, 1)
                if u in MEANS_AT:
                    pool_means(MEANS_AT[u])
                if u in SUMS_AT:
                    pool_sums(IN1 + 6 + SUMS_AT[u] // 2, SUMS_AT[u] % 2)
                if u in POOL_AT:
                    g = POOL_AT[u]
                    dve.wait_ge(pool_hi, g + 1)
                    dve.scalar_tensor_tensor(chunk(g_lo, 4 + g), ps[:, g, :], col("pool", g),
                                             low_of(chunk(g_hi, 4 + g)), ALU.mult, ALU.subtract)\
                       .then_inc(pool_ready, 1)

            def update(n, e, par, m):
                dve.wait_ge(mm_done, 2 * n + e + 1)
                dve.tensor_tensor(chunk(xT, m), chunk(xT, m), bank(par, e), ALU.add).then_inc(evacuated, 1)

            def update_norm(n0, r, gain):
                with dve.Fori(0, 2) as i:
                    for j in range(2):
                        n = n0 + 2 * i + j
                        for e in range(2):
                            update(n, e, n0 + j, 4 * i + 2 * j + e)
                        for e in range(2):
                            dve.wait_ge(evacuated, 2 * n + e + 1)
                            if gain == "final":
                                add_squares(r, 4 * i + 2 * j + e, sq[:, e, :])
                            else:
                                norm_low(r, 4 * i + 2 * j + e, e, gain)

            def ffn(base, r, second):
                done = FC if second else 0
                norm_factor(r)
                for gi, (n0, nd, f0, nf) in enumerate(ffn_plan(base)):
                    with dve.Fori(0, nf // 2) as i:
                        for j in range(2):
                            n = n0 + 2 * i + j
                            f = done + f0 + j + 2 * i
                            off = 2 if second else 0
                            for e in range(2):
                                take_in(n, e, n0 + j, f_in[:, 2 * e + j, off:off + T])
                            if second:
                                c = f0 + j + 2 * i
                                for tap in range(2):
                                    for e in range(2):
                                        o = f_cv[:, 2 * e + j, :]
                                        if tap:
                                            dve.wait_ge(f_tap_vec, 4 * (f - FC) + e + 1)
                                        else:
                                            dve.wait_ge(evacuated, 2 * n + e + 1)
                                            dve.wait_ge(f_tap_act, 2 * (f - FC) + e + 1)
                                        dve.scalar_tensor_tensor(
                                            o, f_in[:, 2 * e + j, 1 - tap:1 - tap + T],
                                            col(f"fconv{1 - tap}", c + FC * e), o, ALU.mult, ALU.add)\
                                           .then_inc(f_tap_vec, 1)
                                dve.wait_ge(f_tap_vec, 4 * (f - FC) + 4)
                            else:
                                dve.wait_ge(evacuated, 2 * n + 2)
                            t = f_cv if second else f_in
                            gate, up = t[:, j, 0:T], t[:, 2 + j, 0:T]
                            dve.wait_ge(f_silu, f + 1)
                            dve.tensor_tensor(up, gate, up, ALU.mult).then_inc(f_prod, 1)
                            dve.wait_ge(f_hi, f + 1)
                            dve.tensor_tensor(chunk(g_lo, 2 * i + j), up, low_of(chunk(g_hi, 2 * i + j)),
                                              ALU.subtract).then_inc(f_ready, 1)
                    if gi < len(GROUPS) - 1:
                        with dve.Fori(0, 2) as i:
                            for j in range(2):
                                for e in range(2):
                                    update(nd + 2 * i + j, e, nd + j, 4 * i + 2 * j + e)
                    else:
                        update_norm(nd, 4 if second else 2, "final" if second else "mix")

            update_norm(OUT1, 1, "norm2")
            ffn(FFN1, 1, False)

            norm_factor(2)
            dve.memset(cz[:, :, 0:2], 0.0).then_inc(pads_cleared, 1)
            for n in range(3):
                for m in range(2):
                    j = 2 * n + m
                    take_in(IN2 + n, m, IN2 + n, q2[:, j, :] if j < 4 else (k2[:, 0, :] if j == 4 else v2_t))
            dve.wait_ge(in2_biased, 5)
            dve.tensor_copy(k2[0:HD, 1, :], k2[HD:P, 0, :])
            dve.tensor_copy(k2[HD:P, 1, :], k2[0:HD, 0, :]).then_inc(k2_ready, 1)
            for m in range(2):
                take_in(IN2 + 3, m, IN2 + 3, cb[:, m, :])
            dve.wait_ge(v_turned, 5)
            dve.tensor_copy(v2[:, :, :], ps[:, 6, :].rearrange("p (n c) -> p n c", n=4)).then_inc(v_ready, 1)
            dve.wait_ge(pads_cleared, 2)
            dve.wait_ge(mask_ready, 1)

            def conv_stage(c, stage):
                m, y = c % 2, cy[:, c % 2, :]
                if stage == 0:
                    dve.wait_ge(in2_biased, 6 + c + 1)
                    dve.scalar_tensor_tensor(cz[:, m, 2:2 + T], cc[:, c, :], col("b_in", 10 + c), cx[:, m, :],
                                             ALU.add, ALU.mult).then_inc(cz_ready, 1)
                elif stage == 1:
                    dve.wait_ge(cz_ready, c + 1)
                    dve.wait_ge(tap_act, c + 1)
                    for tap in range(2):
                        if tap:
                            dve.wait_ge(tap_vec, 2 * c + 1)
                        dve.scalar_tensor_tensor(y, cz[:, m, 1 - tap:1 - tap + T], col("conv", 4 * (1 - tap) + c), y,
                                                 ALU.mult, ALU.add).then_inc(tap_vec, 1)
                elif stage == 2:
                    dve.wait_ge(tap_vec, 2 * c + 2)
                    dve.wait_ge(evacuated, 2 * (IN2 + (8 if c >= 2 else 3)) + m + 1)
                    dve.scalar_tensor_tensor(y, cb[:, c, :], col("b_in", 6 + c), y, ALU.add, ALU.mult)\
                       .then_inc(conv_gated, 1)
                else:
                    dve.wait_ge(conv_hi, c + 1)
                    dve.wait_ge(conv_gated, c + 1)
                    dve.tensor_tensor(chunk(g_lo, 4 + c), y, low_of(chunk(g_hi, 4 + c)), ALU.subtract)\
                       .then_inc(conv_ready, 1)

            for u in range(SPAN + AFTER):
                g = UNITS + u
                if u < UNITS:
                    h, bs = unit2(u)
                    dve.wait_ge(scores_done, g + 1)
                    dve.wait_ge(probs_turned, g - 3)
                    negated_scores(g, p2, [mask2[:, int(b > 0), :] for b in bs], HD ** -0.5,
                                   neg_sink[:, h:h + 1])
                if 1 <= u <= UNITS:
                    normalise(g - 1, p2)
                if u >= 6 and u % 4 == 2:
                    a = (u - 6) // 4
                    dve.wait_ge(heads_hi, 4 + a + 1)
                    dve.tensor_tensor(chunk(g_lo, a), ps[:, 7, :], low_of(chunk(g_hi, a)), ALU.subtract)\
                       .then_inc(heads_ready, 1)
                for c, at in enumerate(CONV_AT):
                    if u in at:
                        conv_stage(c, at.index(u))
                for n, m, k in BESIDE2[u]:
                    if k == KC - 2:
                        part, half = CONV_PART[n]
                        take_in(n, m, n, (cb[:, 2 * half + m, :], cc[:, 2 * half + m, :], cx[:, m, :])[part])

            def take_branches(m):
                n = MIX2 + 2 * m
                for e in range(2):
                    dve.wait_ge(mm_done, 2 * n + e + 1)
                    dve.tensor_copy(branch[:, e, :], bank(MIX2, e)).then_inc(evacuated, 1)

            def merge(m):
                n = MIX2 + 2 * m + 1
                for e in range(2):
                    take_in(n, e, MIX2 + 1, gates[:, e, :])
                for e in range(2):
                    dve.wait_ge(gate_done, 2 * m + e + 1)
                    dve.tensor_tensor(branch[:, e, :], branch[:, e, :], gates[:, e, :], ALU.mult).then_inc(mix_step, 1)
                dve.wait_ge(mix_step, 3 * m + 2)
                dve.tensor_tensor(chunk(merged, m), branch[:, 0, :], branch[:, 1, :], ALU.add).then_inc(mix_step, 1)
                dve.wait_ge(mix_step, 3 * m + 3)

            def merged_low(m):
                dve.wait_ge(merged_hi, m + 1)
                dve.tensor_tensor(chunk(g_lo, m), chunk(merged, m), low_of(chunk(g_hi, m)), ALU.subtract)\
                   .then_inc(merged_ready, 1)

            with dve.Fori(0, KC - 1) as i:
                take_branches(i)
                merge(i)
            take_branches(KC - 1)
            for m in range(KC - 1):
                merged_low(m)
            merge(KC - 1)
            merged_low(KC - 1)

            update_norm(OUT2, 3, "ffn")
            dve.memset(f_in[:, :, 0:2], 0.0).then_inc(pads_cleared, 1)
            dve.wait_ge(pads_cleared, 3)
            ffn(FFN2, 3, True)
            dve.wait_ge(norm_rooted, 5)
            dve.reciprocal(rs_col[:, :], rms_col[:, :]).then_inc(rs_ready, 1)
            dve.wait_ge(rs_ready, 5)
            for t in range(NT):
                dve.wait_ge(y_turned, t + 1)
                dve.tensor_scalar(y_out[:, t, 512:1024], ps[:, 2 * (t % 3) + 1, :], rs_col[:, t:t + 1], None,
                                  ALU.mult).then_inc(y_vec, 1)

        @block.tensor
        def _(pe):
            def step(par, blocks, k, operands, first, last, banks=None):
                for m in blocks:
                    x_hi, x_lo = operands(m, k)
                    w = slice(m * HALF + k * P, m * HALF + (k + 1) * P)
                    wh, wl = w_hi[:, par, w], w_lo[:, par, w]
                    for i, (a, b) in enumerate(((wh, x_hi), (wh, x_lo), (wl, x_hi))):
                        ins = pe.matmul(bank(par if banks is None else banks, m), a, b, start=first and i == 0, stop=last and i == 2)
                    if last:
                        ins.then_inc(mm_done, 1)

            def open_block(n, m):
                pe.wait_ge(w_lo_ready, 2 * n + m + 1)
                if not static(n) or n >= 2:
                    pe.wait_ge(evacuated, 2 * n + m - 3)

            def of(hi, lo):
                return lambda m, k: (hi[:, k * T:(k + 1) * T], lo[:, k * T:(k + 1) * T])

            H, G = of(h_hi, h_lo), of(g_hi, g_lo)

            def panel(n, par, operands, ready=None, base=0, order=range(KC)):
                order = list(order)
                for blocks in ([(0, 1)] if ready is not None else [(0,), (1,)]):
                    for m in blocks:
                        open_block(n, m)
                    for a, k in enumerate(order):
                        if ready is not None:
                            pe.wait_ge(ready, base + k + 1)
                        step(par % 2, blocks, k, operands, a == 0, a == len(order) - 1)

            def norm_sum(r):
                pe.wait_ge(sq_added, KC * (r + 1))
                pe.matmul(ps[:, 4, :], ones[:, :], sq_sum[:, :], start=True, stop=True).then_inc(norm_summed, 1)

            pe.wait_ge(const_step, 2)
            pe.wait_ge(norm1_landed, 16)
            pe.transpose(ps[:, 5, 0:KC], vec_rows[0:KC, 0, :], ident[0:KC, 0:KC]).then_inc(norm1_turned, 1)
            for m in range(KC):
                if m >= 4:
                    pe.wait_ge(x_ready, m - 3)
                for t in range(NT):
                    if m == 0:
                        pe.wait_ge(x_landed[t], 16)
                    ins = pe.transpose(ps[:, m % 4, t * P:(t + 1) * P], x_in[:, t, m * P:(m + 1) * P], ident[:, :])
                ins.then_inc(x_turned, 1)

            def qk_sum(n):
                for c in (2 * n, 2 * n + 1):
                    pe.wait_ge(qk_squared, c + 1)
                    if c >= 2:
                        pe.wait_ge(qk_rooted, c - 1)
                    pe.matmul(ps[:, 5 + c % 2, :], head_ones[:, :], p1[:, c % 2, :], start=True, stop=True)\
                      .then_inc(qk_summed, 1)

            def turn_v(a):
                pe.wait_ge(evacuated, 2 * (4 + a // 2) + a % 2 + 1)
                if a == 0:
                    pe.wait_ge(qk_rooted, 8)
                if a >= 2:
                    pe.wait_ge(v_ready, a - 1)
                for j in range(4):
                    ins = pe.transpose(ps[:, 6 + a % 2, j * P:(j + 1) * P], v_t[:, a % 2, j * P:(j + 1) * P], ident[:, :])
                ins.then_inc(v_turned, 1)

            def block(n, m):
                open_block(n, m)
                for k in range(KC):
                    step(n % 2, [m], k, H, k == 0, k == KC - 1)

            for m in range(2):
                open_block(0, m)
            for k in range(KC):
                pe.wait_ge(h_ready, k + 1)
                step(0, (0, 1), k, H, k == 0, k == KC - 1, banks=-1)
            pe.wait_ge(x_ready, KC)
            block(1, 0)
            pe.wait_ge(vec_landed, 16 * (len(vec_loads) + 4))
            at = 0
            for tile, rows in enumerate(V_ROWS):
                ins = pe.transpose(ps[:, 5, at:at + rows], vec_rows[0:rows, tile, :], ident[0:rows, 0:rows])
                at += rows
            ins.then_inc(vec_turned, 1)
            norm_sum(0)
            block(1, 1)
            pe.wait_ge(const_step, 4)
            panel(2, 2, H)
            qk_sum(0)
            for n in (3, 4):
                block(n, 0)
                qk_sum(n - 2)
                block(n, 1)
            pe.wait_ge(vec_ready, 1)
            qk_sum(3)
            for m in range(2):
                open_block(5, m)
                for k in range(KC):
                    step(1, [m], k, H, k == 0, k == KC - 1)
                    if (m, k) == (1, 4):
                        turn_v(0)
                        turn_v(1)

            def turn_probs(u, p):
                pe.wait_ge(probs_ready, u + 1)
                if u:
                    pe.wait_ge(pt_ready, u)
                for j in range(4):
                    ins = pe.transpose(ps[:, 6, j * P:(j + 1) * P], probs(p, u)[:, j * P:(j + 1) * P], ident[:, :])
                ins.then_inc(probs_turned, 1)

            def values(u, h, bs, pt, value, keys):
                pe.wait_ge(pt_ready, u + 1)
                if u % 4 == 0 and u:
                    pe.wait_ge(heads_ready, u // 4)
                rows = slice(HD * (h % 2), HD * (h % 2) + HD)
                for i, b in enumerate(bs):
                    seen = [(s, j) for s, j in enumerate(keys(b)) if j >= 0]
                    for s, j in seen:
                        ins = pe.matmul(ps[rows, 7, b * P:(b + 1) * P], value(h, j),
                                        pt[:, u % 2, (2 * i + s) * P:(2 * i + s + 1) * P],
                                        start=(s, j) == seen[0], stop=(s, j) == seen[-1])
                ins.then_inc(pv_done, 1)

            def beside_unit(steps):
                for n, m, k in steps:
                    if k == 0:
                        open_block(n, m)
                    for kk in (k, k + 1):
                        step(n % 2, [m], kk, H, kk == 0, kk == KC - 1)

            for u in range(SPAN):
                if u == 0:
                    beside_unit(BESIDE1[u])
                    pe.wait_ge(qk_ready, 8)
                if u < UNITS:
                    h, bs = unit1(u)
                    if u >= 2:
                        pe.wait_ge(scores_read, u - 1)
                    r = slice(HD * (h % 2), HD * (h % 2) + HD)
                    for i, b in enumerate(bs):
                        keys = by_chunk(k1[r, h // 2, :])
                        keys = keys[:, b - 1:b + 1] if b else keys[:, 0:4:3]
                        ins = pe.matmul(ps[:, 4 + u % 2, i * 256:(i + 1) * 256],
                                        q1[r, h // 2, b * P:(b + 1) * P], keys, start=True, stop=True)
                    ins.then_inc(scores_done, 1)
                if u:
                    beside_unit(BESIDE1[u])
                else:
                    turn_v(2)
                    turn_v(3)
                    pe.wait_ge(pool_w_landed, 16)
                if u in POOL_AT:
                    g = POOL_AT[u]
                    pe.wait_ge(pool_in, g + 1)
                    pe.matmul(ps[:, g, :], w_pool_sb[:, g, :], u_pad[:, g % 2, PAD:PAD + T], start=True,
                              stop=True).then_inc(pool_mm, 1)
                if 2 <= u < UNITS + 2:
                    if u == 2:
                        pe.wait_ge(v_ready, 4)
                    turn_probs(u - 2, p1)
                if u >= LAG:
                    values(u - LAG, *unit1(u - LAG), pt1, lambda h, j: v1[:, j, h * HD:(h + 1) * HD], keys1)

            def panels(n0, pairs, operands, order=None, first=0):
                order = list(order or range(KC))
                with pe.Fori(first, pairs) as i:
                    for j in range(2):
                        panel(n0 + 2 * i + j, n0 + j, operands, order=order)

            pe.wait_ge(pool_ready, 4)
            for m in range(2):
                open_block(OUT1, m)
            for a, k in enumerate([4, 5, 6, 7, 0, 1, 2, 3]):
                if k == 0:
                    pe.wait_ge(heads_ready, 3)
                if k == 3:
                    pe.wait_ge(heads_ready, 4)
                step(0, (0, 1), k, G, a == 0, a == KC - 1)
            panel(OUT1 + 1, 1, G)
            panels(OUT1, 2, G, first=1)

            def ffn(base, r, done):
                for gi, (n0, nd, f0, nf) in enumerate(ffn_plan(base)):
                    if gi == 0:
                        panel(n0, n0, H, h_ready, KC * r)
                        norm_sum(r)
                        panel(n0 + 1, n0 + 1, H)
                    panels(n0, nf // 2, H, first=0 if gi else 1)
                    panel(nd, nd, G, f_ready, done + f0, range(nf))
                    panel(nd + 1, nd + 1, G, order=range(nf))
                    panels(nd, 2, G, range(nf), first=1)

            ffn(FFN1, 1, 0)

            panel(IN2, IN2, H, h_ready, 2 * KC)
            norm_sum(2)
            panel(IN2 + 1, IN2 + 1, H)
            panel(IN2 + 2, IN2 + 2, H)
            for m in range(2):
                open_block(IN2 + 3, m)
                for k in range(KC):
                    step((IN2 + 3) % 2, [m], k, H, k == 0, k == KC - 1)
            pe.wait_ge(in2_biased, 6)
            for j in range(4):
                ins = pe.transpose(ps[:, 6, j * P:(j + 1) * P], v2_t[:, j * P:(j + 1) * P], ident[:, :])
            ins.then_inc(v_turned, 1)
            pe.wait_ge(k2_ready, 1)
            for u in range(SPAN):
                g = UNITS + u
                if u < UNITS:
                    h, bs = unit2(u)
                    pe.wait_ge(scores_read, g - 1)
                    r = slice(HD * (h % 2), HD * (h % 2) + HD)
                    keys = k2[r, 0 if h // 4 == h % 2 else 1, :]
                    for i, b in enumerate(bs):
                        kk = keys[:, (b - 1) * P:(b + 1) * P] if b else twice(keys[:, 0:P])
                        ins = pe.matmul(ps[:, 4 + g % 2, i * 256:(i + 1) * 256],
                                        q2[r, h // 2, b * P:(b + 1) * P], kk, start=True, stop=True)
                    ins.then_inc(scores_done, 1)
                if 2 <= u < UNITS + 2:
                    if u == 2:
                        pe.wait_ge(v_ready, 5)
                    turn_probs(g - 2, p2)
                if u >= LAG:
                    values(g - LAG, *unit2(u - LAG), pt2,
                           lambda h, j: v2[:, j, h // 4 * HD:(h // 4 + 1) * HD], lambda b: (b - 1, b))
                beside_unit(BESIDE2[u])

            def branches(n):
                for m in range(2):
                    if static(n):
                        pe.wait_ge((heads_ready, conv_ready)[m], (8, 4)[m])
                    open_block(n, m)
                    for k in range(4):
                        step(MIX2 % 2, [m], k, lambda m, k: G(m, 4 * m + k), k == 0, k == 3)

            branches(MIX2)
            panel(MIX2 + 1, MIX2 + 1, H)
            with pe.Fori(1, KC) as i:
                branches(MIX2 + 2 * i)
                panel(MIX2 + 2 * i + 1, MIX2 + 1, H)

            panel(OUT2, OUT2, G, merged_ready)
            panel(OUT2 + 1, OUT2 + 1, G)
            panels(OUT2, 2, G, first=1)
            ffn(FFN2, 3, FC)

            def turn_y(t):
                for k in range(KC):
                    ins = pe.transpose(ps[:, 2 * (t % 3) + k // 4, (k % 4) * P:(k % 4 + 1) * P],
                                       yT[:, k * T + t * P:k * T + (t + 1) * P], ident[:, :])
                ins.then_inc(y_turned, 1)

            pe.wait_ge(y_scaled, KC)
            pe.wait_ge(evacuated, 2 * PANELS)
            turn_y(0)
            pe.wait_ge(sq_added, 5 * KC)
            for t in range(NT):
                ins = pe.matmul(ps[:, 6, t:t + 1], sq_sum[:, t * P:(t + 1) * P], ones[:, 0:1], start=True, stop=True)
            ins.then_inc(norm_summed, 1)
            turn_y(1)
            turn_y(2)
            pe.wait_ge(y_vec, 1)
            pe.wait_ge(y_act, 1)
            turn_y(3)


_INS = ["x", "norm1_g", "w_in", "q_norm_g", "k_norm_g", "rpb", "w_pool", "pool_scale", "w_out", "norm2_g",
        "w_gate", "w_up", "w_down", "mix_norm_2", "w_in_2", "b_in_2", "sinks_2", "conv_w_2",
        "w_attn_branch_2", "w_conv_branch_2", "w_out_2", "ffn_norm_2", "w_up_2", "ffn_conv_w_2",
        "w_down_2", "final_norm_2"]


def kernel(**inputs):
    import numpy as np
    import concourse.bacc as bacc
    from concourse.bass_utils import run_bass_kernel_spmd

    nc = bacc.Bacc("TRN2", target_bir_lowering=False, num_devices=1)
    arrays, args = {}, []
    for name in _INS:
        a = np.ascontiguousarray(inputs[name])
        arrays["in_" + name] = a
        args.append(nc.dram_tensor("in_" + name, a.shape, mybir.dt.from_np(a.dtype), kind="ExternalInput").ap())
    shape = inputs["x"].shape
    args.append(nc.dram_tensor("out_0", shape, F32, kind="ExternalOutput").ap())
    two_blocks(nc, *args)
    r = run_bass_kernel_spmd(nc, [arrays], core_ids=[0])
    return r.results[0]["out_0"]
```
